# Optimizing a Trainium2 kernel written in Bass

```python
import jax
import jax.numpy as jnp
from jax import lax
import numpy as np

D_MODEL = 1024
BATCH = 1
SEQ = 256
DEPTH = 2

HEAD_DIM = 64
ROPE_THETA = 10000.0
NORM_EPS = 1e-6
Q_BLOCK = 128
NEG_INF = -1e30

NSA_Q_HEADS = 8
NSA_KV_HEADS = 2
NSA_GROUP = NSA_Q_HEADS // NSA_KV_HEADS
N_BRANCH = 3
CMP_LEN = 32
CMP_STRIDE = 16
CMP_HIDDEN = 256
SLC_LEN = 64
SLC_TOPN = 16
WIN_LEN = 512
FORCE_BONUS = 1e4

DIL_PAIRS = ((128, 1), (512, 4), (2048, 16))
DIL_N_GROUPS = len(DIL_PAIRS)
DIL_HEADS_PER_GROUP = 4
DIL_SLOT_HEADS = DIL_N_GROUPS * DIL_HEADS_PER_GROUP
DIL_MAX_WINDOW = max(w for w, _ in DIL_PAIRS)

SB_HEADS = D_MODEL // HEAD_DIM

D_FF = 2816
CONV_WIDTH = 3

NSA_Q_COLS = NSA_Q_HEADS * HEAD_DIM
NSA_KV_COLS = 2 * N_BRANCH * NSA_KV_HEADS * HEAD_DIM
NSA_GATE_COLS = NSA_Q_HEADS * N_BRANCH
DIL_COLS = 3 * DIL_SLOT_HEADS * HEAD_DIM
EVEN_IN = NSA_Q_COLS + NSA_KV_COLS + NSA_GATE_COLS + DIL_COLS
EVEN_OUT = NSA_Q_HEADS * HEAD_DIM + DIL_HEADS_PER_GROUP * HEAD_DIM
ODD_IN = 3 * SB_HEADS * HEAD_DIM
ODD_OUT = SB_HEADS * HEAD_DIM

kernel_name = 'hybrid_nsa_dilated_stickbreaking_convffn'

def rmsnorm(x, g):
    xf = x.astype(jnp.float32)
    y = xf * lax.rsqrt(jnp.mean(xf * xf, axis=-1, keepdims=True) + NORM_EPS)
    return (y * g.astype(jnp.float32)).astype(x.dtype)

def rope(x, pos):
    half = x.shape[-1] // 2
    inv = jnp.power(ROPE_THETA, -jnp.arange(half, dtype=jnp.float32) / half)
    ang = pos.astype(jnp.float32)[:, None] * inv[None, :]
    cos = jnp.cos(ang)[:, None, :]
    sin = jnp.sin(ang)[:, None, :]
    xf = x.astype(jnp.float32)
    x1, x2 = xf[..., :half], xf[..., half:]
    return jnp.concatenate([x1 * cos - x2 * sin, x2 * cos + x1 * sin], axis=-1).astype(x.dtype)

def masked_softmax(s, mask):
    s = jnp.where(mask, s, NEG_INF)
    return jax.nn.softmax(s, axis=-1) * mask

def compress_blocks(x_raw, pe, w1, w2):
    B, S, G, D = x_raw.shape
    nc = (S - CMP_LEN) // CMP_STRIDE + 1
    idx = jnp.arange(nc)[:, None] * CMP_STRIDE + jnp.arange(CMP_LEN)[None, :]
    blocks = x_raw[:, idx] + pe[:, None, :]
    blocks = jnp.moveaxis(blocks, 3, 2).reshape(B, nc, G, CMP_LEN * D)
    return jax.nn.gelu(blocks @ w1, approximate=True) @ w2

def cmp_to_slc_overlap(n_cmp, n_slc):
    cs = np.arange(n_cmp) * CMP_STRIDE
    ss = np.arange(n_slc) * SLC_LEN
    lo = np.maximum(cs[:, None], ss[None, :])
    hi = np.minimum(cs[:, None] + CMP_LEN, ss[None, :] + SLC_LEN)
    return (np.maximum(hi - lo, 0) / CMP_LEN).astype(np.float32)

def nsa_attention(q, k_cmp, v_cmp, k_slc, v_slc, k_win, v_win, gates):
    B, S, Hq, D = q.shape
    G, Hg = NSA_KV_HEADS, NSA_GROUP
    nc = k_cmp.shape[1]
    ns = S // SLC_LEN
    top_n = min(SLC_TOPN, ns)
    scale = D ** -0.5
    cmp_end = jnp.arange(nc) * CMP_STRIDE + CMP_LEN - 1
    overlap = jnp.asarray(cmp_to_slc_overlap(nc, ns))
    kbs = k_slc.reshape(B, ns, SLC_LEN, G, D).transpose(0, 3, 1, 2, 4)
    vbs = v_slc.reshape(B, ns, SLC_LEN, G, D).transpose(0, 3, 1, 2, 4)
    kw_pad = jnp.pad(k_win, ((0, 0), (WIN_LEN, 0), (0, 0), (0, 0)))
    vw_pad = jnp.pad(v_win, ((0, 0), (WIN_LEN, 0), (0, 0), (0, 0)))
    b_ix = jnp.arange(B)[:, None, None, None]
    g_ix = jnp.arange(G)[None, :, None, None]
    blk = jnp.arange(ns)

    def block(qb):
        s0 = qb * Q_BLOCK
        t = s0 + jnp.arange(Q_BLOCK)
        qt = lax.dynamic_slice_in_dim(q, s0, Q_BLOCK, 1).reshape(B, Q_BLOCK, G, Hg, D)
        gt = lax.dynamic_slice_in_dim(gates, s0, Q_BLOCK, 1).reshape(B, Q_BLOCK, G, Hg, N_BRANCH)
        sc = jnp.einsum('btghd,bngd->bghtn', qt, k_cmp).astype(jnp.float32) * scale
        pc = masked_softmax(sc, cmp_end[None, :] <= t[:, None])
        o_c = jnp.einsum('bghtn,bngd->btghd', pc.astype(v_cmp.dtype), v_cmp)
        imp = jnp.einsum('bghtn,nj->bgtj', pc, overlap)
        cur = t // SLC_LEN
        forced = (blk[None, :] == 0) | (blk[None, :] == cur[:, None]) | (blk[None, :] == cur[:, None] - 1)
        future = blk[None, :] * SLC_LEN > t[:, None]
        imp = jnp.where(future, -1.0, imp) + jnp.where(forced, FORCE_BONUS, 0.0)
        _, idx = lax.top_k(imp, top_n)
        ks = kbs[b_ix, g_ix, idx]
        vs = vbs[b_ix, g_ix, idx].reshape(B, G, Q_BLOCK, top_n * SLC_LEN, D)
        kpos = (idx[..., None] * SLC_LEN + jnp.arange(SLC_LEN)).reshape(B, G, 1, Q_BLOCK, top_n * SLC_LEN)
        ss = jnp.einsum('btghd,bgtnld->bghtnl', qt, ks).astype(jnp.float32)
        ss = ss.reshape(B, G, Hg, Q_BLOCK, top_n * SLC_LEN) * scale
        ps = masked_softmax(ss, kpos <= t[:, None])
        o_s = jnp.einsum('bghtm,bgtmd->btghd', ps.astype(vs.dtype), vs)
        kw = lax.dynamic_slice_in_dim(kw_pad, s0, WIN_LEN + Q_BLOCK, 1)
        vw = lax.dynamic_slice_in_dim(vw_pad, s0, WIN_LEN + Q_BLOCK, 1)
        kp = s0 - WIN_LEN + jnp.arange(WIN_LEN + Q_BLOCK)
        dist = t[:, None] - kp[None, :]
        wmask = (dist >= 0) & (dist < WIN_LEN) & (kp[None, :] >= 0)
        sw = jnp.einsum('btghd,bkgd->bghtk', qt, kw).astype(jnp.float32) * scale
        pw = masked_softmax(sw, wmask)
        o_w = jnp.einsum('bghtk,bkgd->btghd', pw.astype(vw.dtype), vw)
        o = gt[..., 0:1] * o_c + gt[..., 1:2] * o_s + gt[..., 2:3] * o_w
        return o.reshape(B, Q_BLOCK, Hq * D).astype(q.dtype)

    out = lax.map(block, jnp.arange(S // Q_BLOCK))
    return jnp.moveaxis(out, 0, 1).reshape(B, S, Hq * D)

def dilated_attention(q, k, v):
    B, S, _, D = q.shape
    NG, HG = DIL_N_GROUPS, DIL_HEADS_PER_GROUP
    scale = D ** -0.5
    pad = DIL_MAX_WINDOW
    q = q.reshape(B, S, NG, HG, D)
    kp = jnp.pad(k, ((0, 0), (pad, 0), (0, 0), (0, 0))).reshape(B, S + pad, NG, HG, D)
    vp = jnp.pad(v, ((0, 0), (pad, 0), (0, 0), (0, 0))).reshape(B, S + pad, NG, HG, D)
    k_groups = [kp[:, :, g] for g in range(NG)]
    v_groups = [vp[:, :, g] for g in range(NG)]

    def block(qb):
        s0 = qb * Q_BLOCK
        t = s0 + jnp.arange(Q_BLOCK)
        qt = lax.dynamic_slice_in_dim(q, s0, Q_BLOCK, 1)
        outs, lses = [], []
        for g, (window, dil) in enumerate(DIL_PAIRS):
            offs = jnp.arange(window // dil + 1) * dil
            kpos = t[:, None] - offs[None, :]
            kg = k_groups[g][:, kpos + pad]
            vg = v_groups[g][:, kpos + pad]
            s = jnp.einsum('bthd,btkhd->bhtk', qt[:, :, g], kg).astype(jnp.float32) * scale
            s = jnp.where(kpos >= 0, s, NEG_INF)
            lse = jax.nn.logsumexp(s, axis=-1)
            p = jnp.exp(s - lse[..., None])
            outs.append(jnp.einsum('bhtk,btkhd->bthd', p.astype(vg.dtype), vg))
            lses.append(lse)
        alpha = jax.nn.softmax(jnp.stack(lses), axis=0)
        alpha = jnp.transpose(alpha, (0, 1, 3, 2))[..., None]
        o = jnp.sum(alpha * jnp.stack(outs), axis=0)
        return o.reshape(B, Q_BLOCK, HG * D).astype(q.dtype)

    out = lax.map(block, jnp.arange(S // Q_BLOCK))
    return jnp.moveaxis(out, 0, 1).reshape(B, S, HG * D)

def stick_breaking_attention(q, k, v):
    B, S, H, D = q.shape
    scale = D ** -0.5
    s_idx = jnp.arange(S)

    def block(qb):
        s0 = qb * Q_BLOCK
        t = s0 + jnp.arange(Q_BLOCK)
        qt = lax.dynamic_slice_in_dim(q, s0, Q_BLOCK, 1)
        z = jnp.einsum('bthd,bshd->bhts', qt, k).astype(jnp.float32) * scale
        strict = s_idx[None, :] < t[:, None]
        log_beta = jax.nn.log_sigmoid(z)
        log_1mb = jnp.where(strict, log_beta - z, 0.0)
        after = lax.cumsum(log_1mb, axis=3, reverse=True) - log_1mb
        a = jnp.where(strict, jnp.exp(log_beta + after), 0.0)
        o = jnp.einsum('bhts,bshd->bthd', a.astype(v.dtype), v)
        return o.reshape(B, Q_BLOCK, H * D).astype(q.dtype)

    out = lax.map(block, jnp.arange(S // Q_BLOCK))
    return jnp.moveaxis(out, 0, 1).reshape(B, S, H * D)

def even_mixer(h, w_in, w_out, cmp_pe, cmp_w1, cmp_w2):
    B, S, _ = h.shape
    proj = h @ w_in
    o1 = NSA_Q_COLS
    o2 = o1 + NSA_KV_COLS
    o3 = o2 + NSA_GATE_COLS
    pos = jnp.arange(S)
    nsa_q = rope(proj[..., :o1].reshape(B, S, NSA_Q_HEADS, HEAD_DIM), pos)
    kv = proj[..., o1:o2].reshape(B, S, 2 * N_BRANCH, NSA_KV_HEADS, HEAD_DIM)
    gates = jax.nn.sigmoid(proj[..., o2:o3].astype(jnp.float32)).reshape(B, S, NSA_Q_HEADS, N_BRANCH)
    nc = (S - CMP_LEN) // CMP_STRIDE + 1
    cmp_end = jnp.arange(nc) * CMP_STRIDE + CMP_LEN - 1
    k_cmp = rope(compress_blocks(kv[:, :, 0], cmp_pe[0], cmp_w1[0], cmp_w2[0]), cmp_end)
    v_cmp = compress_blocks(kv[:, :, 1], cmp_pe[1], cmp_w1[1], cmp_w2[1])
    k_slc = rope(kv[:, :, 2], pos)
    k_win = rope(kv[:, :, 4], pos)
    o_nsa = nsa_attention(nsa_q, k_cmp, v_cmp, k_slc, kv[:, :, 3], k_win, kv[:, :, 5], gates)
    dil = proj[..., o3:].reshape(B, S, 3, DIL_SLOT_HEADS, HEAD_DIM)
    o_dil = dilated_attention(rope(dil[:, :, 0], pos), rope(dil[:, :, 1], pos), dil[:, :, 2])
    return jnp.concatenate([o_nsa, o_dil], axis=-1) @ w_out

def odd_mixer(h, w_in, w_out):
    B, S, _ = h.shape
    qkv = (h @ w_in).reshape(B, S, 3, SB_HEADS, HEAD_DIM)
    return stick_breaking_attention(qkv[:, :, 0], qkv[:, :, 1], qkv[:, :, 2]) @ w_out

def conv_ffn(h, w_up, conv_w, conv_b, w_down):
    S = h.shape[1]
    u = h @ w_up
    up = jnp.pad(u, ((0, 0), (CONV_WIDTH - 1, 0), (0, 0)))
    c = conv_b
    for tap in range(CONV_WIDTH):
        c = c + conv_w[tap] * up[:, tap:tap + S]
    gate, val = jnp.split(c, 2, axis=-1)
    return (jax.nn.gelu(gate, approximate=True) * val) @ w_down

def setup_inputs(seed: int = 0) -> dict:
    key = jax.random.key(seed)
    ks = jax.random.split(key, 13)
    n_even = (DEPTH + 1) // 2
    n_odd = DEPTH // 2
    f32 = jnp.float32

    def w(k, shape, fan_in):
        return jax.random.normal(k, shape, f32) * fan_in ** -0.5

    return {
        'x': jax.random.normal(ks[0], (BATCH, SEQ, D_MODEL), f32),
        'norm_g': 1.0 + 0.05 * jax.random.normal(ks[1], (DEPTH, 4, D_MODEL), f32),
        'even_w_in': w(ks[2], (n_even, D_MODEL, EVEN_IN), D_MODEL),
        'even_w_out': w(ks[3], (n_even, EVEN_OUT, D_MODEL), EVEN_OUT),
        'cmp_pe': 0.02 * jax.random.normal(ks[4], (n_even, 2, CMP_LEN, HEAD_DIM), f32),
        'cmp_w1': w(ks[5], (n_even, 2, CMP_LEN * HEAD_DIM, CMP_HIDDEN), CMP_LEN * HEAD_DIM),
        'cmp_w2': w(ks[6], (n_even, 2, CMP_HIDDEN, HEAD_DIM), CMP_HIDDEN),
        'odd_w_in': w(ks[7], (n_odd, D_MODEL, ODD_IN), D_MODEL),
        'odd_w_out': w(ks[8], (n_odd, ODD_OUT, D_MODEL), ODD_OUT),
        'ffn_w_up': w(ks[9], (DEPTH, D_MODEL, 2 * D_FF), D_MODEL),
        'ffn_conv_w': w(ks[10], (DEPTH, CONV_WIDTH, 2 * D_FF), CONV_WIDTH),
        'ffn_conv_b': 0.02 * jax.random.normal(ks[11], (DEPTH, 2 * D_FF), f32),
        'ffn_w_down': w(ks[12], (DEPTH, D_FF, D_MODEL), D_FF),
    }

def reference(x, norm_g, even_w_in, even_w_out, cmp_pe, cmp_w1, cmp_w2, odd_w_in, odd_w_out,
              ffn_w_up, ffn_conv_w, ffn_conv_b, ffn_w_down):
    h = x
    for layer in range(DEPTH):
        i = layer // 2
        y = rmsnorm(h, norm_g[layer, 0])
        if layer % 2 == 0:
            y = even_mixer(y, even_w_in[i], even_w_out[i], cmp_pe[i], cmp_w1[i], cmp_w2[i])
        else:
            y = odd_mixer(y, odd_w_in[i], odd_w_out[i])
        h = h + rmsnorm(y, norm_g[layer, 1])
        y = conv_ffn(rmsnorm(h, norm_g[layer, 2]), ffn_w_up[layer], ffn_conv_w[layer],
                     ffn_conv_b[layer], ffn_w_down[layer])
        h = h + rmsnorm(y, norm_g[layer, 3])
    return h


_drawn_inputs = setup_inputs


def setup_inputs(seed=0):
    import zlib

    import numpy as np

    out = dict(_drawn_inputs(seed))
    spreads = {}
    factors = {}
    for name, (base, spread) in spreads.items():
        noise = np.random.default_rng([zlib.crc32(name.encode()), seed]).standard_normal(out[name].shape)
        drawn = base * np.exp(spread * noise) if base else spread * noise
        out[name] = jnp.asarray(drawn.astype(out[name].dtype))
    for name, factor in factors.items():
        out[name] = (out[name] * factor).astype(out[name].dtype)
    return out
```

```python
from contextlib import ExitStack

import numpy as np

import concourse.bass as bass
from concourse import mybir

F32 = mybir.dt.float32
F32R = mybir.dt.float32r
BF16 = mybir.dt.bfloat16
ALU = mybir.AluOpType
ACT = mybir.ActivationFunctionType
AX = mybir.AxisListType

P = 128
SEQ = 256
TT = SEQ // P
D = 1024
KT = D // P
HD = 64
EPS = 1e-6
NEG = -1e30

NSA_HEADS = 8
NSA_G = 2
NSA_PER = NSA_HEADS // NSA_G
BRANCH = 3
CMP_LEN = 32
CMP_STRIDE = 16
NC = (SEQ - CMP_LEN) // CMP_STRIDE + 1
NCP = 16
CM = P // NCP
CMP_H = 256
CKT = CMP_LEN * HD // P
DIL = (1, 4, 16)
DIL_WINDOW = (128, 512, 2048)
NG = len(DIL)
SLOTS = 4
D_FF = 2816
FT = D_FF // P
TAPS = 3
SB_HEADS = 16
SCALE = HD ** -0.5

BLK = 512
UNIT = 4 * BLK
RING = 4
LOOK = 2

UP_CHUNKS = 2 * FT * P // BLK
EVEN_KT = (NSA_HEADS + SLOTS) * HD // P
STAGES = [("in0", 7 * 2 + 4), ("out0", 2 * EVEN_KT // 4), ("up0", UP_CHUNKS * 2), ("down0", 2 * FT // 4),
          ("in1", 6 * 2), ("out1", 2 * KT // 4), ("up1", UP_CHUNKS * 2), ("down1", 2 * FT // 4)]
FIRST_UNIT = {}
NUNITS = 0
for _name, _n in STAGES:
    FIRST_UNIT[_name] = NUNITS
    NUNITS += _n

TQ, TDQ, TDK, TSLC, TWIN = 0, 4, 10, 16, 17
V_KC, V_VC, V_SLC, V_WIN, V_DIL = 0, 128, 256, 384, 512
TABLES, LATE = 3, 6


def build(nc, x, weights, wgate, cmpw2, pe2, gpre, gpost, convw, rope, ropec, cmask, blocks, masks, identf, tri,
          out):
    ctx = ExitStack()
    with ctx:
        def sem(name):
            return ctx.enter_context(nc.semaphore(name))

        def sb(name, shape, dt=F32, c=ctx):
            return c.enter_context(nc.sbuf_tensor(name, shape, dt))

        h = sb("h", [P, TT, D])
        xn = sb("xn", [P, TT, D])
        xhi = sb("xhi", [P, KT, SEQ], F32R)
        xlo = sb("xlo", [P, KT, SEQ], F32R)
        raw = sb("raw", [P, RING, UNIT])
        whi = sb("whi", [P, RING, UNIT], F32R)
        wlo = sb("wlo", [P, RING, UNIT], F32R)
        c_gpre = sb("c_gpre", [P, D])
        c_gpost = sb("c_gpost", [P, D])
        c_conv = sb("c_conv", [P, 2 * UP_CHUNKS * 4 * 4])
        c_rope = sb("c_rope", [P, 2, 2, TT, HD])
        c_ropec = sb("c_ropec", [2 * NC, 2, HD])
        c_cmask = sb("c_cmask", [P, 2, TT, NC])
        c_mask = sb("c_mask", [P, NG + 1, SEQ], BF16)
        c_identf = sb("c_identf", [P, P])
        c_identb = sb("c_identb", [P, P], BF16)
        c_tri = sb("c_tri", [P, 2, P])
        c_wg = sb("c_wg", [P, KT, NSA_HEADS * BRANCH])
        wg_hi = sb("wg_hi", [P, KT, NSA_HEADS * BRANCH], F32R)
        wg_lo = sb("wg_lo", [P, KT, NSA_HEADS * BRANCH], F32R)
        c_w2 = sb("c_w2", [P, 2, 2, HD])
        c_pe2 = sb("c_pe2", [P, 2, CKT])
        meanh = sb("meanh", [P, 2, TT, 2])
        ms = sb("ms", [P, 2, TT])
        rstd = sb("rstd", [P, 2, TT])
        mhalf = sb("mhalf", [P, 1])

        a = ctx.enter_context(ExitStack())
        vbuf = sb("vbuf", [P, TT, 1280], F32, a)
        qkT = sb("qkT", [P, 18, SEQ], F32, a)
        gates = sb("gates", [P, TT, NSA_HEADS * BRANCH], F32, a)
        kcT = sb("kcT", [P, 2 * NC], F32, a)
        vc = sb("vc", [P, CM, HD], F32, a)
        stat = sb("stat", [P, 3, 8], F32, a)
        coef = sb("coef", [P, 2, 8], F32, a)
        stc = sb("stc", [P, 3, TT * CM], F32, a)
        pcm = sb("pcm", [P, TT * CM, NCP], F32, a)
        pcT = sb("pcT", [P, TT, P], F32, a)
        blockd = sb("c_blockd", [P, CM], F32, a)
        b = a.enter_context(ExitStack())
        t12 = sb("t12", [P, 2, TT, BLK], F32, b)
        mask_f = t12[:, 0, :, :].rearrange("p t (m c) -> p (t m) c", c=SEQ)
        x2 = sb("x2", [P, 4, P], F32, b)
        xbf = sb("xbf", [P, 2, CKT * 2 * NC], F32, b)
        xb_hi = sb("xb_hi", [P, 2, CKT * 2 * NC + P], F32R, b)
        xb_lo = sb("xb_lo", [P, 2, CKT * 2 * NC + P], F32R, b)
        hid = sb("hid", [2 * NC, 2, CMP_H], F32, b)
        hidT = sb("hidT", [P, 2, 2 * NC], F32, b)
        hidR = sb("hidR", [P, 2, CM, NCP], F32, b)
        kcr = sb("kcr", [2 * NC, 4, HD], F32, b)
        b.close()
        b = a.enter_context(ExitStack())
        probs = sb("probs", [P, 2, 1024], F32, b)
        probsT = sb("probsT", [P, 2, 1024], F32, b)
        b.close()
        sb_sp = sb("sb_sp", [P, 2, 2, 384], F32, b)
        sb_a = sb("sb_a", [P, 2, 2, 384], F32, b)
        b.close()
        a.close()
        hid_hi = sb("hid_hi", [P, FT, SEQ], F32R, a)
        hid_lo = sb("hid_lo", [P, FT, SEQ], F32R, a)
        conv = sb("conv", [P, 2, 4, SEQ], F32, a)
        act_g = sb("act_g", [P, 2, 2, SEQ], F32, a)
        hidf = sb("hidf", [P, 2, 2, SEQ], F32, a)

        ps = ctx.enter_context(nc.psum_tensor("ps", [P, 8, BLK], F32))
        psq = ps[:, :, :].rearrange("p b (q c) -> p (b q) c", c=P)
        psh = ps[:, :, :].rearrange("p b (q c) -> p (b q) c", c=SEQ)

        ident_in, gpre_in, gpost_in, wg_in, tables_in, late_in = (
            sem(s + "_in") for s in ("ident", "gpre", "gpost", "wg", "tables", "late"))
        x_in = [sem(f"x_in{t}") for t in range(TT)]
        out_done = sem("out_done")
        raw_in = [sem(f"raw_in{s}") for s in range(RING)]
        hi_done, lo_done, unit_used = sem("hi_done"), sem("lo_done"), sem("unit_used")
        half_set, mask_cast = sem("half_set"), sem("mask_cast")
        pre_sq, pre_ms, pre_rstd, pre_xn, pre_tr, pre_hi, pre_lo = (
            sem("pre_" + s) for s in ("sq", "ms", "rstd", "xn", "tr", "hi", "lo"))
        y_done = [sem(f"y_done{t}") for t in range(TT)]
        post_sq, post_ms, post_rstd, post_yg, post_h = (
            sem(s) for s in ("post_sq", "post_ms", "post_rstd", "post_yg", "post_h"))
        in_free_act = sem("in_free_act")
        rope_parts, staged, turned, turned_out = sem("rope_parts"), sem("staged"), sem("turned"), sem("turned_out")
        wg_done, gate_ready, gate_tanh, gate_done = (sem(s) for s in ("wg_done", "gate_ready", "gate_tanh", "gate_done"))
        x2_turned, x2_out, xb_pad, xb_sum, xb_hid, xb_split = (
            sem(s) for s in ("x2_turned", "x2_out", "xb_pad", "xb_sum", "xb_hid", "xb_split"))
        hid_gelu, hid_turned, hid_out = (sem(s) for s in ("hid_gelu", "hid_turned", "hid_out"))
        cmp_ready, kc_prod, kc_rot, vc_out, kc_turned, kc_out = (
            sem(s) for s in ("cmp_ready", "kc_prod", "kc_rot", "vc_out", "kc_turned", "kc_out"))
        cs_ready, cs_step, cs_exp, pc_turned, pc_out, oc_ready, oc_out = (
            sem(s) for s in ("cs_ready", "cs_step", "cs_exp", "pc_turned", "pc_out", "oc_ready", "oc_out"))
        vc_zero, vc_ready = sem("vc_zero"), sem("vc_ready")
        it_scores, it_max, it_exp, it_coef, it_turned, it_pT0, it_pT1, it_pv, it_o, ot_turned, ot_hi, ot_lo = (
            sem("it_" + s) for s in ("scores", "max", "exp", "coef", "turned", "pT0", "pT1", "pv", "o", "ot_turned",
                                     "ot_hi", "ot_lo"))
        sb_z, sb_absd, sb_exp1, sb_ln, sb_spd, sb_cum, sb_prob, sb_pv, sb_ohi, sb_olo = (
            sem("sb_" + s) for s in ("z", "absd", "exp1", "ln", "spd", "cum", "prob", "pv", "ohi", "olo"))
        up_ident, up_tap1, up_free, up_gelu, up_hf, up_hi, up_lo = (
            sem("up_" + s) for s in ("ident", "tap1", "free", "gelu", "hf", "hi", "lo"))

        EVEN_STEPS = [("unit", 0, 0), ("unit", 0, 1), ("gate",), ("unit", 1, 0), ("x2T",), ("unit", 1, 1),
                      ("unit", 2, 0), ("turn", 1), ("unit", 2, 1), ("cmp1", 0, 0), ("cmp1", 0, 1),
                      ("unit", 3, 0), ("turn", 2), ("unit", 3, 1), ("cmp1", 1, 0), ("cmp1", 1, 1),
                      ("unit", 4, 0), ("turn", 3), ("hidT",), ("unit", 4, 1), ("cmp2",), ("unit", 5, 0),
                      ("turn", 4), ("kcT",), ("unit", 5, 1), ("cscore",), ("unit", 6, 0), ("turn", 5),
                      ("unit", 6, 1)]
        ODD_STEPS = [("unit", 0, 0), ("unit", 0, 1), ("unit", 1, 0), ("turn", 0), ("unit", 1, 1), ("unit", 2, 0),
                     ("turn", 1), ("unit", 2, 1), ("unit", 3, 0), ("turn", 2), ("unit", 3, 1), ("unit", 4, 0),
                     ("turn", 3), ("unit", 4, 1), ("unit", 5, 0), ("unit", 5, 1)]
        EVEN_ACT = 3
        EVEN_ROT = 5

        ITEMS = [("dil", j, t) for j in range(SLOTS) for t in range(TT)] + \
                [("nsa", i, t) for i in range(NSA_PER) for t in range(TT)]
        NI = len(ITEMS)
        TURNS = [n for n, (kind, j, _) in enumerate(ITEMS) if kind == "nsa" or j % 2]
        PC_TURN, PC_VALUES = 2, (4, 6)
        NP = SB_HEADS // 2

        def s_half(n):
            return 4 * ((n + 1) % 2)

        TILE_OF = [NSA_PER + j // 2 if kind == "dil" else j for kind, j, _ in ITEMS]

        def turns_before(n):
            return sum(1 for m in TURNS if m < n)

        def wide_before(n):
            return sum(1 for m in range(n) if ITEMS[m][2])

        def ends(steps, first):
            u, found = first, {}
            for step in steps:
                if step[0] in ("unit", "cmp1"):
                    u += 1
                    if step[2] == 1:
                        found[step[:2]] = u
            return found

        EVEN_END, ODD_END = ends(EVEN_STEPS, FIRST_UNIT["in0"]), ends(ODD_STEPS, FIRST_UNIT["in1"])
        TILE_MAJOR = [(c, t) for t in range(TT) for c in range(2)]
        HALF_MAJOR = [(c, t) for c in range(2) for t in range(TT)]
        Y_ORDER = [TILE_MAJOR, HALF_MAJOR, HALF_MAJOR, HALF_MAJOR]
        Y_BANK = (0, 4, 0, 4)
        T_BANK = (4, 4, 0, 4)

        def colhalf(c):
            return slice(c * BLK, (c + 1) * BLK)

        def maps_of(n):
            return NG if ITEMS[n][0] == "dil" else 4

        block = ctx.enter_context(nc.Block())

        @block.sync
        def _(sp):
            for t in range(TT):
                sp.dma_start(h[:, t, :], x[t * P:(t + 1) * P, :]).then_inc(x_in[t], 16)
            for u in range(RING):
                sp.dma_start(raw[:, u, :], weights[u]).then_inc(raw_in[u], 16)
            rounds = (NUNITS - RING) // RING
            with sp.Fori(0, rounds) as i:
                for s in range(RING):
                    sp.wait_ge(lo_done, RING * i + (s + 1))
                    sp.dma_start(raw[:, s, :], weights[bass.ds(RING * i + (RING + s), 1)]
                                 .rearrange("u p n -> (u p) n")).then_inc(raw_in[s], 16)
            for u in range(RING + rounds * RING, NUNITS):
                sp.wait_ge(lo_done, u - RING + 1)
                sp.dma_start(raw[:, u % RING, :], weights[u]).then_inc(raw_in[u % RING], 16)
            for t in range(TT):
                sp.wait_ge(post_h, 2 * (3 * TT + t + 1))
                sp.dma_start(out[t * P:(t + 1) * P, :], h[:, t, :]).then_inc(out_done, 16)
            sp.wait_ge(out_done, 16 * TT)

        @block.scalar
        def _(act):
            def load_gain(dst, src, p, signal):
                act.dma_start(dst[:], src[p:p + 1, :].partition_broadcast(P)
                              .rearrange("p a n -> p (a n)")).then_inc(signal, 16)

            def load(signal, *pairs):
                for dst, src in pairs:
                    act.dma_start(dst, src).then_inc(signal, 16)

            load_gain(c_gpre, gpre, 0, gpre_in)
            load(ident_in, (c_identf[:], identf))
            load(wg_in, (c_wg[:], wgate))

            def split(slot, at, wait_used):
                act.wait_ge(raw_in[slot], 16 * at[1])
                if wait_used:
                    act.wait_ge(unit_used, at[0] - (RING - 1))
                act.copy(whi[:, slot, :], raw[:, slot, :]).then_inc(hi_done, 1)

            def split_ahead(u):
                v = u + LOOK
                if v < NUNITS:
                    split(v % RING, (v, v // RING + 1), v >= RING)

            def pre(p, between=None):
                for t in range(TT):
                    for c in range(2):
                        if p == 0:
                            act.wait_ge(x_in[t], 16)
                        else:
                            act.wait_ge(post_h, 2 * ((p - 1) * TT + t) + c + 1)
                        act.activation(xn[:, t, colhalf(c)], h[:, t, colhalf(c)], ACT.Square, scale=D ** -0.5,
                                       accum_out=meanh[:, 0, t, c:c + 1]).then_inc(pre_sq, 1)
                    if p > 0:
                        pre_his(p, t)
                        if t == 0:
                            post_squares(p - 1, 1)
                if p == 0:
                    split(0, (0, 1), False)
                    for t in range(TT):
                        pre_his(p, t)
                    split(1, (1, 1), False)
                if p in (0, 1, 2):
                    act.wait_ge(pre_xn, 2 * TT * (p + 1))
                    load_gain(c_gpre, gpre, p + 1, gpre_in)
                if p > 0:
                    load_gain(c_gpost, gpost, p, gpost_in)

            def pre_his(p, t):
                for c in range(2):
                    act.wait_ge(pre_tr, 2 * (p * TT + t) + c + 1)
                    act.copy(xhi[:, 4 * c:4 * c + 4, t * P:(t + 1) * P],
                             ps[:, T_BANK[p] + 2 * t + c, :].rearrange("p (k c) -> p k c", c=P)).then_inc(pre_hi, 1)

            def post_squares(p, part):
                order = Y_ORDER[p]
                cut = 2 if p == 0 else 3
                for c, t in order[:cut] if part == 0 else order[cut:]:
                    act.wait_ge(y_done[t], 2 * p + c + 1)
                    act.activation(xn[:, t, colhalf(c)], ps[:, Y_BANK[p] + 2 * t + c, :], ACT.Square,
                                   scale=D ** -0.5, accum_out=meanh[:, 1, t, c:c + 1]).then_inc(post_sq, 1)

            def plain_stage(name):
                for u in range(FIRST_UNIT[name], FIRST_UNIT[name] + dict(STAGES)[name]):
                    split_ahead(u)

            pre(0)
            load(tables_in, (c_rope[:], rope), (mask_f, masks), (c_pe2[:], pe2))
            load(late_in, (c_w2[:], cmpw2), (c_ropec[:], ropec), (c_cmask[:], cmask), (blockd[:], blocks), (c_tri[:], tri),
                 (c_conv[:], convw))
            load_gain(c_gpost, gpost, 0, gpost_in)
            act.wait_ge(wg_in, 16)
            act.copy(wg_hi[:], c_wg[:]).then_inc(wg_done, 1)

            u = FIRST_UNIT["in0"]
            for step in EVEN_STEPS:
                if step[0] in ("unit", "cmp1"):
                    split_ahead(u)
                    u += 1
                if step == ("unit", 0, 1):
                    act.wait_ge(unit_used, EVEN_END["unit", 0])
                    for t in range(TT):
                        src = ps[:, t, 0:4 * HD].rearrange("p (k d) -> p k d", d=HD).unsqueeze(2)
                        act.copy(xn[:, 0, t * BLK:(t + 1) * BLK].rearrange("p (k e d) -> p k e d", e=2, d=HD),
                                 src.to_broadcast([P, 4, 2, HD]))
                    act.copy(vbuf[:, :, V_SLC:BLK], ps[:, 0:2, V_SLC:BLK]).then_inc(in_free_act, 1)
                elif step == ("gate",):
                    act.wait_ge(gate_ready, 1)
                    act.activation(gates[:], ps[:, 7, 0:TT * 24].rearrange("p (t c) -> p t c", t=TT), ACT.Tanh,
                                   scale=0.5).then_inc(gate_tanh, 1)
                elif step == ("x2T",):
                    act.wait_ge(x2_turned, 1)
                    for par in range(2):
                        v = psh[par * HD:(par + 1) * HD, 12:16, :].rearrange("p k (m two) -> p k m two", two=2)
                        act.copy(x2[par * HD:(par + 1) * HD, :, :], v[:, :, :, par]).then_inc(x2_out, 1)
                    act.wait_ge(xb_sum, 4)
                    act.copy(xb_hi[:, :, 0:CKT * 2 * NC], xbf[:]).then_inc(xb_hid, 1)
                elif step[0] == "turn":
                    c = step[1]
                    n = 2 if c == 5 else 4
                    act.wait_ge(turned, c)
                    act.copy(qkT[:, 4 * (c - 1):4 * (c - 1) + n, :], psh[:, 8:8 + n, :]).then_inc(turned_out, 1)
                elif step == ("cmp1", 1, 1):
                    act.wait_ge(unit_used, EVEN_END["cmp1", 1])
                    act.activation(hid[:], ps[0:2 * NC, 6:8, 0:CMP_H], ACT.Gelu_apprx_tanh).then_inc(hid_gelu, 1)
                elif step == ("unit", 5, 1):
                    act.wait_ge(unit_used, EVEN_END["unit", 5])
                    act.wait_ge(rope_parts, TT * 5)
                    act.copy(vbuf[:, :, 512:768], ps[:, 2:4, 256:512]).then_inc(in_free_act, 1)
                elif step == ("unit", 6, 1):
                    act.wait_ge(unit_used, EVEN_END["unit", 6])
                    act.copy(vbuf[:, :, 768:1280], ps[:, 0:2, :]).then_inc(in_free_act, 1)
                    act.wait_ge(cs_step, 4)
                    act.activation(pcm[:, :, 0:NC], pcm[:, :, 0:NC], ACT.Exp).then_inc(cs_exp, 1)

            def it_probs(n):
                kind, _, t = ITEMS[n]
                s, w, o, v = n % 2, P * (t + 1), s_half(n), n % 3
                act.wait_ge(it_max, n + 1)
                if n >= 2:
                    act.wait_ge(it_turned, n - 1)
                if kind == "dil":
                    act.activation(probs[:, s, 0:NG * w].rearrange("p (m c) -> p m c", c=w),
                                   psh[:, o:o + NG, 0:w], ACT.Exp, bias=stat[:, v, 0:1],
                                   accum_out=stat[:, v, 4:5]).then_inc(it_exp, 1)
                else:
                    for m in range(4):
                        act.activation(probs[:, s, m * w:(m + 1) * w], psh[:, o + m, 0:w], ACT.Exp,
                                       bias=stat[:, v, m:m + 1], accum_out=stat[:, v, 4 + m:5 + m]).then_inc(it_exp, 1)

            def it_turned_out(n):
                k = min(BLK, maps_of(n) * (ITEMS[n][2] + 1) * P)
                act.wait_ge(it_turned, n + 1)
                if n >= 2:
                    act.wait_ge(it_pv, n - 1)
                act.copy(probsT[:, n % 2, 0:k], ps[:, 4, 0:k]).then_inc(it_pT0, 1)

            def it_hi(n):
                tile = TILE_OF[n]
                act.wait_ge(ot_turned, turns_before(n) + 1)
                act.copy(xhi[:, tile, ITEMS[n][2] * P:(ITEMS[n][2] + 1) * P], ps[:, 6 + n % 2, 384:512]).then_inc(ot_hi, 1)

            it_probs(0)
            for n in range(NI + 2):
                if n + 1 < NI:
                    it_probs(n + 1)
                if n < NI:
                    it_turned_out(n)
                if n - 2 in TURNS:
                    it_hi(n - 2)
            plain_stage("out0")
            post_squares(0, 0)

            def ffn(layer):
                pre(2 * layer + 1)
                act.wait_ge(late_in, 16 * LATE)
                act.preload_act_table_set("gelu_apprx_tanh_and_others")
                u0, k0 = FIRST_UNIT[f"up{layer}"], layer * UP_CHUNKS

                def identities(par, at, cofs):
                    act.wait_ge(unit_used, u0 + 2 + 2 * at)
                    for bank in range(2):
                        for m in (2 * bank, 2 * bank + 1):
                            act.activation(conv[:, par, m, :], psh[:, 4 * par + m, :], ACT.Identity,
                                           scale=c_conv[:, bass.ds(cofs + (4 * m + 2), 1)],
                                           bias=c_conv[:, bass.ds(cofs + (4 * m + 3), 1)]).then_inc(up_ident, 1)

                def gelu(par, at):
                    act.wait_ge(up_free, 1 + k0 + 1 + at)
                    act.activation(act_g[:, par], conv[:, par, 0:2, :], ACT.Gelu_apprx_tanh).then_inc(up_gelu, 1)

                def hidden_hi(par, at, tile):
                    act.wait_ge(up_hf, 1 + k0 + 1 + at)
                    act.copy(hid_hi[:, tile, :], hidf[:, par]).then_inc(up_hi, 1)

                split_ahead(u0)
                split_ahead(u0 + 1)
                identities(0, 0, layer * UP_CHUNKS * 16)
                with act.Fori(0, (UP_CHUNKS - 1) // 2) as i:
                    for j in range(2):
                        par = (1 + j) % 2
                        for half in range(2):
                            v = u0 + 2 + 2 * j + half + LOOK
                            split(v % RING, (4 * i + v, i + (v // RING + 1)), True)
                        gelu(1 - par, 2 * i + j)
                        if j == 0:
                            act.wait_ge(up_hf, 1 + k0 + 2 * i)
                        else:
                            act.wait_ge(up_hf, 1 + k0 + 2 * i + 1)
                        identities(par, 2 * i + (1 + j), (2 * i + (1 + j)) * 16 + layer * UP_CHUNKS * 16)
                        hidden_hi(1 - par, 2 * i + j, bass.ds(4 * i + 2 * j, 2))
                last = UP_CHUNKS - 1
                gelu(last % 2, last)
                hidden_hi(last % 2, last, slice(2 * last, 2 * last + 2))
                plain_stage(f"down{layer}")
                post_squares(2 * layer + 1, 0)

            ffn(0)

            pre(2)
            u = FIRST_UNIT["in1"]
            for step in ODD_STEPS:
                if step[0] == "unit":
                    split_ahead(u)
                    u += 1
                    if step[2] == 1:
                        c = step[1]
                        act.wait_ge(unit_used, ODD_END["unit", c])
                        if c < 4:
                            if c >= 2:
                                act.wait_ge(turned, EVEN_ROT + c - 1)
                            act.copy(xn[:, c % 2, :].rearrange("p (t c) -> p t c", t=TT),
                                     ps[:, 2 * (c % 2):2 * (c % 2) + 2, :]).then_inc(in_free_act, 1)
                        else:
                            act.copy(vbuf[:, :, (c - 4) * BLK:(c - 3) * BLK],
                                     ps[:, 2 * (c % 2):2 * (c % 2) + 2, :]).then_inc(in_free_act, 1)

            act.preload_act_table_set("natural_log_exp_and_others")

            def sb_soft(n):
                s = n % 2
                act.wait_ge(sb_z, n + 1)
                if n >= 2:
                    act.wait_ge(sb_cum, n - 1)
                act.activation(sb_sp[:, s], ps[:, 2 * (n % 3):2 * (n % 3) + 2, 0:384], ACT.Abs).then_inc(sb_absd, 1)
                act.wait_ge(sb_absd, n + 1)
                act.activation(sb_sp[:, s], sb_sp[:, s], ACT.Exp, scale=-1.0).then_inc(sb_exp1, 1)
                act.wait_ge(sb_exp1, n + 1)
                act.activation(sb_sp[:, s], sb_sp[:, s], ACT.Ln, bias=1.0).then_inc(sb_ln, 1)

            def sb_weights(n):
                act.wait_ge(sb_cum, n + 1)
                if n >= 2:
                    act.wait_ge(sb_pv, n - 1)
                act.activation(sb_a[:, n % 2], ps[:, 2 * (n % 3):2 * (n % 3) + 2, 0:384], ACT.Exp).then_inc(sb_prob, 1)

            def sb_hi(n):
                act.wait_ge(sb_pv, n + 1)
                act.copy(xhi[:, n, :], ps[:, 6 + n % 2, 0:SEQ]).then_inc(sb_ohi, 1)

            sb_soft(0)
            for n in range(NP + 1):
                if n + 1 < NP:
                    sb_soft(n + 1)
                if n < NP:
                    sb_weights(n)
                if n >= 1:
                    sb_hi(n - 1)
            plain_stage("out1")
            post_squares(2, 0)
            ffn(1)
            post_squares(3, 1)

        @block.vector
        def _(dve):
            def split(slot, at):
                dve.wait_ge(hi_done, at + 1)
                dve.tensor_tensor(wlo[:, slot, :], raw[:, slot, :], whi[:, slot, :].bitcast(F32),
                                  ALU.subtract).then_inc(lo_done, 1)

            def split_ahead(u):
                v = u + LOOK
                if v < NUNITS:
                    split(v % RING, v)

            def pre_ms_of(p, t):
                dve.wait_ge(pre_sq, 2 * (p * TT + t + 1))
                dve.tensor_scalar(ms[:, 0, t:t + 1], meanh[:, 0, t, 0:1], meanh[:, 0, t, 1:2], EPS, ALU.add,
                                  ALU.add).then_inc(pre_ms, 1)

            def pre_normed(p, t):
                dve.wait_ge(gpre_in, 16 * (p + 1))
                dve.wait_ge(pre_rstd, p * TT + t + 1)
                for c in range(2):
                    dve.scalar_tensor_tensor(xn[:, t, colhalf(c)], h[:, t, colhalf(c)], rstd[:, 0, t:t + 1],
                                             c_gpre[:, colhalf(c)], ALU.mult, ALU.mult).then_inc(pre_xn, 1)

            def pre_los(p, t):
                tok = slice(t * P, (t + 1) * P)
                for c in range(2):
                    dve.wait_ge(pre_hi, 2 * (p * TT + t) + c + 1)
                    dve.tensor_tensor(xlo[:, 4 * c:4 * c + 4, tok],
                                      ps[:, T_BANK[p] + 2 * t + c, :].rearrange("p (k c) -> p k c", c=P),
                                      xhi[:, 4 * c:4 * c + 4, tok].bitcast(F32), ALU.subtract).then_inc(pre_lo, 1)

            def post_gain(p, t):
                for k, (c, tile) in enumerate(Y_ORDER[p]):
                    if tile != t:
                        continue
                    dve.wait_ge(post_sq, 4 * p + k + 1)
                    dve.tensor_tensor(xn[:, t, colhalf(c)], ps[:, Y_BANK[p] + 2 * t + c, :], c_gpost[:, colhalf(c)],
                                      ALU.mult).then_inc(post_yg, 1)

            def post_residual(p, t):
                k = [i for i, (c, tile) in enumerate(Y_ORDER[p]) if tile == t][-1]
                dve.wait_ge(post_sq, 4 * p + k + 1)
                dve.tensor_scalar(ms[:, 1, t:t + 1], meanh[:, 1, t, 0:1], meanh[:, 1, t, 1:2], EPS, ALU.add,
                                  ALU.add).then_inc(post_ms, 1)
                post_gain(p, t)
                dve.wait_ge(post_yg, 2 * (TT * p + t + 1))
                dve.wait_ge(post_rstd, TT * p + t + 1)
                for c in range(2):
                    dve.scalar_tensor_tensor(h[:, t, colhalf(c)], xn[:, t, colhalf(c)], rstd[:, 1, t:t + 1],
                                             h[:, t, colhalf(c)], ALU.mult, ALU.add).then_inc(post_h, 1)

            def junction(p):
                dve.wait_ge(gpost_in, 16 * (p + 1))
                for t in range(TT):
                    post_residual(p, t)
                    if p < 3:
                        pre_ms_of(p + 1, t)
                        pre_normed(p + 1, t)
                        pre_los(p + 1, t)

            for t in range(TT):
                pre_ms_of(0, t)
            for t in range(TT):
                pre_normed(0, t)
            pre_los(0, 0)
            split(0, 0)
            pre_los(0, 1)
            split(1, 1)
            dve.wait_ge(wg_done, 1)
            dve.tensor_tensor(wg_lo[:], c_wg[:], wg_hi[:].bitcast(F32), ALU.subtract).then_inc(wg_done, 1)

            dve.wait_ge(tables_in, 16 * TABLES)
            dve.wait_ge(mask_cast, 1)

            def rotate(c):
                bank = 2 * (c % 2)
                dve.wait_ge(unit_used, EVEN_END["unit", c])
                if c >= 2:
                    dve.wait_ge(staged, TT * (c - 1))
                parts = {1: [(0, 8, 0)], 2: [(0, 8, 0)], 3: [(0, 4, 0), (4, 8, 1)], 4: [(0, 8, 1)], 5: [(0, 4, 1)]}[c]
                for t in range(TT):
                    src = ps[:, bank + t, :].rearrange("p (h d) -> p h d", d=HD)
                    t1 = t12[:, 0, t, :].rearrange("p (h d) -> p h d", d=HD)
                    t2 = t12[:, 1, t, :].rearrange("p (h d) -> p h d", d=HD)
                    half = HD // 2
                    for lo, hi, which in parts:
                        n = hi - lo
                        cos = c_rope[:, which, 0, t, :].unsqueeze(1).to_broadcast([P, n, HD])
                        sin = c_rope[:, which, 1, t, :].unsqueeze(1)
                        dve.tensor_tensor(t1[:, lo:hi, :], src[:, lo:hi, :], cos, ALU.mult)
                        dve.tensor_tensor(t2[:, lo:hi, 0:half], src[:, lo:hi, half:HD],
                                          sin[:, :, 0:half].to_broadcast([P, n, half]), ALU.mult)
                        ins = dve.tensor_tensor(t2[:, lo:hi, half:HD], src[:, lo:hi, 0:half],
                                                sin[:, :, half:HD].to_broadcast([P, n, half]), ALU.mult)
                    ins.then_inc(rope_parts, 1)

            u = FIRST_UNIT["in0"]
            for step in EVEN_STEPS:
                if step[0] in ("unit", "cmp1"):
                    split_ahead(u)
                    u += 1
                if step[0] == "unit" and step[2] == 1 and 1 <= step[1] <= 5:
                    rotate(step[1])
                elif step == ("gate",):
                    dve.wait_ge(gate_tanh, 1)
                    dve.tensor_scalar(gates[:], gates[:], 0.5, 0.5, ALU.mult, ALU.add).then_inc(gate_done, 1)
                elif step == ("x2T",):
                    dve.wait_ge(x2_out, 2)
                    for kind in range(2):
                        for g in range(NSA_G):
                            v = x2[:, 2 * kind + g, :].rearrange("p (n k) -> p k n", k=8)
                            dst = xbf[:, kind, :].rearrange("p (k g n) -> p k g n", g=2, n=NC)
                            for kh in range(2):
                                ins = dve.tensor_tensor(
                                    dst[:, 8 * kh:8 * kh + 8, g, :], v[:, :, kh:kh + NC],
                                    c_pe2[:, kind, 8 * kh:8 * kh + 8].unsqueeze(2).to_broadcast([P, 8, NC]), ALU.add)
                            ins.then_inc(xb_sum, 1)
                    dve.wait_ge(xb_hid, 1)
                    dve.tensor_tensor(xb_lo[:, :, 0:CKT * 2 * NC], xbf[:],
                                      xb_hi[:, :, 0:CKT * 2 * NC].bitcast(F32), ALU.subtract).then_inc(xb_split, 1)
                elif step == ("hidT",):
                    dve.wait_ge(hid_turned, 1)
                    dve.tensor_copy(hidT[:], ps[:, 6, 0:2 * 2 * NC].rearrange("p (k n) -> p k n", k=2))
                    dve.wait_ge(vc_zero, 1)
                    for k in range(2):
                        src = ps[:, 6, (2 + k) * 2 * NC:(3 + k) * 2 * NC].rearrange("p (g n) -> p g n", g=2)
                        ins = dve.tensor_copy(
                            hidR[:, k, :, 0:NC].rearrange("p (i g) n -> p i g n", g=2),
                            src.unsqueeze(1).to_broadcast([P, NSA_PER, 2, NC]))
                    ins.then_inc(hid_out, 1)
                elif step == ("cmp2",):
                    dve.wait_ge(late_in, 16 * LATE)
                    dve.wait_ge(cmp_ready, 1)
                    half = HD // 2
                    src = ps[0:2 * NC, 7, 0:HD]
                    dve.tensor_tensor(kcr[:, 2, :], src, c_ropec[:, 0, :], ALU.mult)
                    dve.tensor_tensor(kcr[:, 3, 0:half], src[:, half:HD], c_ropec[:, 1, 0:half], ALU.mult)
                    dve.tensor_tensor(kcr[:, 3, half:HD], src[:, 0:half], c_ropec[:, 1, half:HD],
                                      ALU.mult).then_inc(kc_prod, 1)
                    dve.wait_ge(kc_prod, 1)
                    for k in range(2):
                        ins = dve.tensor_tensor(kcr[:, k, :], kcr[:, 2, :], kcr[:, 3, :], ALU.add)
                    ins.then_inc(kc_rot, 1)
                    dve.tensor_tensor(vc[:], ps[:, 6, 0:HD].unsqueeze(1).to_broadcast([P, CM, HD]),
                                      blockd[:].unsqueeze(2).to_broadcast([P, CM, HD]), ALU.mult).then_inc(vc_out, 1)
                elif step == ("kcT",):
                    dve.wait_ge(kc_turned, 1)
                    dve.tensor_copy(kcT[:], ps[:, 7, 0:2 * NC]).then_inc(kc_out, 1)
                elif step == ("cscore",):
                    dve.wait_ge(cs_ready, 1)
                    for g in range(NSA_G):
                        for t in range(TT):
                            ins = dve.tensor_tensor(
                                pcm[:, CM * t + g:CM * (t + 1):2, 0:NC],
                                ps[:, 6 + g, 0:P].rearrange("p (k n) -> p k n", n=NCP)[:, 4 * t:4 * t + 4, 0:NC],
                                c_cmask[:, 0, t, :].unsqueeze(1).to_broadcast([P, 4, NC]), ALU.add)
                    ins.then_inc(cs_step, 1)
                    dve.wait_ge(cs_step, 1)
                    dve.tensor_reduce(stc[:, 0, :], pcm[:, :, 0:NC], AX.X, ALU.max).then_inc(cs_step, 1)
                    dve.wait_ge(cs_step, 2)
                    dve.tensor_tensor(pcm[:, :, 0:NC], pcm[:, :, 0:NC],
                                      stc[:, 0, :].unsqueeze(2).to_broadcast([P, TT * CM, NC]),
                                      ALU.subtract).then_inc(cs_step, 2)

            def compressed_probs():
                dve.wait_ge(cs_exp, 1)
                dve.tensor_reduce(stc[:, 1, :], pcm[:, :, 0:NC], AX.X, ALU.add).then_inc(cs_step, 1)
                dve.wait_ge(cs_step, 5)
                dve.reciprocal(stc[:, 1, :], stc[:, 1, :]).then_inc(cs_step, 1)
                dve.wait_ge(cs_step, 6)
                for t in range(TT):
                    gv = gates[:, t, :].rearrange("p (g i b) -> p i g b", g=2, b=BRANCH)[:, :, :, 0]
                    o = slice(CM * t, CM * (t + 1))
                    ins = dve.tensor_tensor(stc[:, 2, o].rearrange("p (i g) -> p i g", g=2),
                                            stc[:, 1, o].rearrange("p (i g) -> p i g", g=2), gv, ALU.mult)
                ins.then_inc(cs_step, 1)
                dve.wait_ge(cs_step, 7)
                dve.tensor_tensor(pcm[:, :, 0:NC], pcm[:, :, 0:NC],
                                  stc[:, 2, :].unsqueeze(2).to_broadcast([P, TT * CM, NC]), ALU.mult).then_inc(cs_step, 1)
                dve.wait_ge(cs_step, 8)
                for t in range(TT):
                    o = slice(CM * t, CM * (t + 1))
                    ins = dve.tensor_tensor(pcm[:, o, 0:NC], pcm[:, o, 0:NC],
                                            c_cmask[:, 1, t, :].unsqueeze(1).to_broadcast([P, CM, NC]), ALU.mult)
                ins.then_inc(cs_step, 1)

            def it_maxima(n):
                kind, _, t = ITEMS[n]
                s, w, o, m = n % 3, P * (t + 1), s_half(n), maps_of(n)
                dve.wait_ge(it_scores, n + 1)
                if kind == "dil":
                    dve.tensor_reduce(stat[:, s, 0:1], psh[:, o:o + m, 0:w], AX.XY, ALU.max,
                                      negate=True).then_inc(it_max, 1)
                else:
                    dve.tensor_reduce(stat[:, s, 0:4], psh[:, o:o + 4, 0:w], AX.X, ALU.max,
                                      negate=True).then_inc(it_max, 1)

            def it_turned_out(n):
                if ITEMS[n][2] == 0:
                    return
                k = maps_of(n) * 2 * P
                dve.wait_ge(it_turned, n + 1)
                if n >= 2:
                    dve.wait_ge(it_pv, n - 1)
                dve.tensor_copy(probsT[:, n % 2, BLK:k], ps[:, 5, 0:k - BLK]).then_inc(it_pT1, 1)

            exps = [sum(1 if ITEMS[k][0] == "dil" else 4 for k in range(n + 1)) for n in range(NI)]
            done = {"coef": 0, "o": 0}

            def it_output(n):
                kind, j, t = ITEMS[n]
                v, s = n % 3, n % 2
                dve.wait_ge(it_exp, exps[n])
                if kind == "dil":
                    dve.reciprocal(coef[:, s, 0:1], stat[:, v, 4:5]).then_inc(it_coef, 1)
                    done["coef"] += 1
                    dve.wait_ge(it_coef, done["coef"])
                    dve.wait_ge(it_pv, n + 1)
                    col = (TILE_OF[n] * 2 + j % 2) * HD
                    dve.tensor_scalar(xn[:, t, col:col + HD], ps[:, 6 + s, 0:HD], coef[:, s, 0:1], None,
                                      ALU.mult).then_inc(it_o, 1)
                    done["o"] += 1
                    return
                dve.reciprocal(coef[:, s, 0:4], stat[:, v, 4:8]).then_inc(it_coef, 1)
                dve.wait_ge(it_coef, done["coef"] + 1)
                gv = gates[:, t, :].rearrange("p (g i b) -> p g i b", g=2, b=BRANCH)[:, :, j, 1:3]
                dve.tensor_tensor(coef[:, s, 4:8].rearrange("p (g b) -> p g b", g=2),
                                  coef[:, s, 0:4].rearrange("p (g b) -> p g b", g=2), gv, ALU.mult).then_inc(it_coef, 1)
                done["coef"] += 2
                dve.wait_ge(it_coef, done["coef"])
                dve.wait_ge(it_pv, n + 1)
                dve.wait_ge(oc_out, t + 1)
                for br in range(2):
                    for g in range(NSA_G):
                        m, col = 2 * g + br, (2 * j + g) * HD
                        ins = dve.scalar_tensor_tensor(xn[:, t, col:col + HD], ps[:, 6 + s, m * HD:(m + 1) * HD],
                                                       coef[:, s, 4 + m:5 + m], xn[:, t, col:col + HD], ALU.mult,
                                                       ALU.add)
                    ins.then_inc(it_o, 1)
                    done["o"] += 1
                    if br == 0:
                        dve.wait_ge(it_o, done["o"])

            def it_lo(n):
                tile, tok = TILE_OF[n], slice(ITEMS[n][2] * P, (ITEMS[n][2] + 1) * P)
                dve.wait_ge(ot_hi, turns_before(n) + 1)
                dve.tensor_tensor(xlo[:, tile, tok], ps[:, 6 + n % 2, 384:512], xhi[:, tile, tok].bitcast(F32),
                                  ALU.subtract).then_inc(ot_lo, 1)

            it_maxima(0)
            for n in range(NI + 2):
                if n + 1 < NI:
                    it_maxima(n + 1)
                if n < NI:
                    it_turned_out(n)
                if n == 0:
                    compressed_probs()
                elif n == PC_TURN:
                    dve.wait_ge(pc_turned, 1)
                    dve.tensor_copy(pcT[:], ps[:, 5, 0:TT * P].rearrange("p (t c) -> p t c", t=TT)).then_inc(pc_out, 1)
                elif n in PC_VALUES:
                    t = PC_VALUES.index(n)
                    dve.wait_ge(oc_ready, t + 1)
                    dve.tensor_copy(xn[:, t, 0:BLK], ps[:, 5, :]).then_inc(oc_out, 1)
                if 1 <= n <= NI:
                    it_output(n - 1)
                if n - 2 in TURNS:
                    it_lo(n - 2)

            def plain_stage(name):
                for u in range(FIRST_UNIT[name], FIRST_UNIT[name] + dict(STAGES)[name]):
                    split_ahead(u)

            plain_stage("out0")
            junction(0)

            def ffn(layer):
                u0, k0 = FIRST_UNIT[f"up{layer}"], layer * UP_CHUNKS

                def taps(par, at, cofs):
                    for bank in range(2):
                        dve.wait_ge(up_ident, 4 * (k0 + at) + 2 * (bank + 1))
                        for m in (2 * bank, 2 * bank + 1):
                            ins = dve.scalar_tensor_tensor(
                                conv[:, par, m, 1:SEQ], psh[:, 4 * par + m, 0:SEQ - 1],
                                c_conv[:, bass.ds(cofs + (4 * m + 1), 1)], conv[:, par, m, 1:SEQ], ALU.mult, ALU.add)
                        ins.then_inc(up_tap1, 1)
                    for bank in range(2):
                        dve.wait_ge(up_tap1, 2 * (k0 + at) + (bank + 1))
                        for m in (2 * bank, 2 * bank + 1):
                            ins = dve.scalar_tensor_tensor(
                                conv[:, par, m, 2:SEQ], psh[:, 4 * par + m, 0:SEQ - 2],
                                c_conv[:, bass.ds(cofs + 4 * m, 1)], conv[:, par, m, 2:SEQ], ALU.mult, ALU.add)
                    ins.then_inc(up_free, 1)

                split_ahead(u0)
                split_ahead(u0 + 1)
                taps(0, 0, layer * UP_CHUNKS * 16)
                with dve.Fori(0, (UP_CHUNKS - 1) // 2) as i:
                    for j in range(2):
                        for half in range(2):
                            v = u0 + 2 + 2 * j + half + LOOK
                            split(v % RING, 4 * i + v)
                        taps((1 + j) % 2, 2 * i + (1 + j), (2 * i + (1 + j)) * 16 + layer * UP_CHUNKS * 16)
                plain_stage(f"down{layer}")
                junction(2 * layer + 1)

            ffn(0)

            u = FIRST_UNIT["in1"]
            for step in ODD_STEPS:
                if step[0] == "unit":
                    split_ahead(u)
                    u += 1
                elif step[0] == "turn":
                    c = step[1]
                    dve.wait_ge(turned, EVEN_ROT + c + 1)
                    b0 = 8 + 4 * (c % 2)
                    dve.tensor_scalar(qkT[:, 4 * c:4 * c + 4, :], psh[:, b0:b0 + 4, :], SCALE if c < 2 else 1.0, None,
                                      ALU.mult).then_inc(turned_out, 1)

            def sb_soft(n):
                s, banks = n % 2, slice(2 * (n % 3), 2 * (n % 3) + 2)
                dve.wait_ge(sb_ln, n + 1)
                dve.scalar_tensor_tensor(sb_sp[:, s], ps[:, banks, 0:384], 0.0, sb_sp[:, s], ALU.max,
                                         ALU.add).then_inc(sb_spd, 1)

            def sb_lo(n):
                dve.wait_ge(sb_ohi, n + 1)
                dve.tensor_tensor(xlo[:, n, :], ps[:, 6 + n % 2, 0:SEQ], xhi[:, n, :].bitcast(F32),
                                  ALU.subtract).then_inc(sb_olo, 1)

            sb_soft(0)
            for n in range(NP + 1):
                if n + 1 < NP:
                    sb_soft(n + 1)
                if n >= 1:
                    sb_lo(n - 1)
            plain_stage("out1")
            junction(2)
            ffn(1)

        @block.gpsimd
        def _(pool):
            pool.memset(mhalf[:], -0.5).then_inc(half_set, 1)
            pool.wait_ge(half_set, 1)
            pool.sem_inc(up_free, 1)
            pool.sem_inc(up_hf, 1)

            def power(p, which, t, ready, done):
                pool.wait_ge(ready, TT * p + t + 1)
                pool.tensor_tensor(rstd[:, which, t:t + 1], ms[:, which, t:t + 1], mhalf[:], ALU.pow).then_inc(done, 1)

            for t in range(TT):
                power(0, 0, t, pre_ms, pre_rstd)
            pool.wait_ge(ident_in, 16)
            pool.wait_ge(tables_in, 16 * TABLES)
            pool.tensor_copy(c_mask[:], mask_f)
            pool.tensor_copy(c_identb[:], c_identf[:]).then_inc(mask_cast, 1)
            pool.memset(xb_hi[:, :, CKT * 2 * NC:].bitcast(F32), 0.0)
            pool.memset(xb_lo[:, :, CKT * 2 * NC:].bitcast(F32), 0.0).then_inc(xb_pad, 1)
            pool.memset(hidR[:, :, :, NC:], 0.0).then_inc(vc_zero, 1)
            pool.memset(pcm[:, :, NC:], 0.0).then_inc(vc_zero, 1)
            for c in range(1, 6):
                n = 256 if c == 5 else 512
                for t in range(TT):
                    pool.wait_ge(rope_parts, TT * (c - 1) + t + 1)
                    if c == 2 and t == 0:
                        pool.wait_ge(x2_turned, 1)
                    if c >= 3 and t == 0:
                        pool.wait_ge(turned, c - 2)
                    pool.tensor_tensor(xn[:, c % 2, t * BLK:t * BLK + n], t12[:, 0, t, 0:n], t12[:, 1, t, 0:n],
                                       ALU.add).then_inc(staged, 1)
            def junction(p):
                for t in range(TT):
                    power(p, 1, t, post_ms, post_rstd)
                    if p < 3:
                        power(p + 1, 0, t, pre_ms, pre_rstd)

            junction(0)

            def ffn(layer):
                k0 = layer * UP_CHUNKS

                def hidden(par, at, tile):
                    pool.wait_ge(up_gelu, k0 + 1 + at)
                    pool.tensor_tensor(hidf[:, par], act_g[:, par], conv[:, par, 2:4, :], ALU.mult).then_inc(up_hf, 1)
                    pool.wait_ge(up_hi, k0 + 1 + at)
                    pool.tensor_tensor(hid_lo[:, tile, :], hidf[:, par], hid_hi[:, tile, :].bitcast(F32),
                                       ALU.subtract).then_inc(up_lo, 1)

                with pool.Fori(0, (UP_CHUNKS - 1) // 2) as i:
                    for j in range(2):
                        hidden(j, 2 * i + j, bass.ds(4 * i + 2 * j, 2))
                last = UP_CHUNKS - 1
                hidden(last % 2, last, slice(2 * last, 2 * last + 2))
                junction(2 * layer + 1)

            ffn(0)
            junction(2)
            ffn(1)

        @block.tensor
        def _(pe):
            def pre(p, t):
                for c in range(2):
                    pe.wait_ge(pre_xn, 2 * (p * TT + t) + c + 1)
                    for k in range(4 * c, 4 * c + 4):
                        ins = pe.transpose(psq[:, 4 * T_BANK[p] + 8 * t + k, :], xn[:, t, k * P:(k + 1) * P], c_identf[:])
                    ins.then_inc(pre_tr, 1)

            def three(out, s_hi, s_lo, m_hi, m_lo, start, stop, shared=False):
                pe.matmul(out, s_hi, m_hi, start=start, stop=False, skip_group_check=shared)
                pe.matmul(out, s_hi, m_lo, start=False, stop=False, skip_group_check=shared)
                return pe.matmul(out, s_lo, m_hi, start=False, stop=stop, skip_group_check=shared)

            def tile_block(slot, b, kt, ohi, olo, t, out, start, stop):
                cols, tok = slice(b * BLK, (b + 1) * BLK), slice(t * P, (t + 1) * P)
                return three(out, ohi[:, kt, tok], olo[:, kt, tok], whi[:, slot, cols], wlo[:, slot, cols], start, stop)

            def token_block(slot, b, kt, ohi, olo, banks, start, stop):
                for t in range(TT):
                    ins = tile_block(slot, b, kt, ohi, olo, t, ps[:, banks[t], :], start, stop)
                return ins

            def in_unit(u, bank, half):
                slot = u % RING
                pe.wait_ge(lo_done, u + 1)
                for b in range(4):
                    kt = 4 * half + b
                    ins = token_block(slot, b, kt, xhi, xlo, (bank, bank + 1), kt == 0, kt == KT - 1)
                ins.then_inc(unit_used, 1)

            def first_units(u0, p):
                for t in range(TT):
                    for kt in range(KT):
                        u, b = u0 + kt // 4, kt % 4
                        if b == 0:
                            pe.wait_ge(pre_lo, 2 * (p * TT + t) + kt // 4 + 1)
                            pe.wait_ge(lo_done, u + 1)
                        ins = tile_block(u % RING, b, kt, xhi, xlo, t, ps[:, t, :], kt == 0, kt == KT - 1)
                        if t == TT - 1 and b == 3:
                            ins.then_inc(unit_used, 1)
                    if t == 0 and p > 0:
                        pre(p, 1)

            def out_proj(name, p, kts, ohi, olo, ready=None):
                u0, y0 = FIRST_UNIT[name], Y_BANK[p]
                tail = 2 * kts - 8

                def block_of(blk, tiles):
                    c, kt, u, b = blk // kts, blk % kts, u0 + blk // 4, blk % 4
                    if b == 0:
                        pe.wait_ge(lo_done, u + 1)
                    if ready is not None and c == 0 and kt % 2 == 0:
                        ready(kt // 2)
                    for t in tiles:
                        ins = tile_block(u % RING, b, kt, ohi, olo, t, ps[:, y0 + 2 * t + c, :], kt == 0, kt == kts - 1)
                        if kt == kts - 1:
                            ins.then_inc(y_done[t], 1)
                    if b == 3 and tiles[-1] == TT - 1:
                        if kt == kts - 1:
                            pe.wait_ge(y_done[TT - 1], 2 * p + c + 1)
                            pe.sem_inc(unit_used, 1)
                        else:
                            ins.then_inc(unit_used, 1)

                for blk in range(tail):
                    block_of(blk, range(TT))
                for t in range(TT):
                    for blk in range(tail, 2 * kts):
                        block_of(blk, (t,))

            pe.wait_ge(ident_in, 16)
            for t in range(TT):
                pre(0, t)

            u = FIRST_UNIT["in0"]
            for step in EVEN_STEPS:
                if step[0] == "unit":
                    c, half = step[1:]
                    if c >= 2 and half == 0:
                        if c == 2:
                            pe.wait_ge(in_free_act, 1)
                        else:
                            pe.wait_ge(rope_parts, TT * (c - 2))
                    if c > 0:
                        in_unit(u, 2 * (c % 2), half)
                    elif half == 1:
                        first_units(u - 1, 0)
                    u += 1
                elif step == ("gate",):
                    pe.wait_ge(wg_done, 2)
                    for kt in range(KT):
                        for t in range(TT):
                            tok = slice(t * P, (t + 1) * P)
                            ins = three(ps[:, 7, t * 24:(t + 1) * 24], xhi[:, kt, tok], xlo[:, kt, tok],
                                        wg_hi[:, kt, :], wg_lo[:, kt, :], kt == 0 and t == 0, kt == KT - 1, True)
                    ins.then_inc(gate_ready, 1)
                elif step == ("x2T",):
                    pe.wait_ge(in_free_act, 1)
                    pe.wait_ge(gate_tanh, 1)
                    for kg in range(4):
                        for t in range(TT):
                            src = xn[:, 0, t * BLK + kg * P:t * BLK + (kg + 1) * P]
                            ins = pe.transpose(psq[:, 24 + 2 * kg + t, :], src, c_identf[:])
                    ins.then_inc(x2_turned, 1)
                elif step[0] == "turn":
                    c = step[1]
                    pe.wait_ge(staged, TT * c)
                    if c >= 2:
                        pe.wait_ge(turned_out, c - 1)
                    for tile in range(2 if c == 5 else 4):
                        for t in range(TT):
                            ins = pe.transpose(psq[:, 16 + 2 * tile + t, :],
                                               xn[:, c % 2, t * BLK + tile * P:t * BLK + (tile + 1) * P], c_identf[:])
                    ins.then_inc(turned, 1)
                elif step[0] == "cmp1":
                    kind, half = step[1:]
                    if half == 0:
                        pe.wait_ge(xb_split, 1)
                        pe.wait_ge(xb_pad, 1)
                    pe.wait_ge(lo_done, u + 1)
                    for b in range(8):
                        kt = 8 * half + b
                        win = slice(kt * 2 * NC, kt * 2 * NC + P)
                        cols = slice(b * CMP_H, (b + 1) * CMP_H)
                        ins = three(ps[:, 6 + kind, 0:CMP_H], xb_hi[:, kind, win], xb_lo[:, kind, win],
                                    whi[:, u % RING, cols], wlo[:, u % RING, cols], kt == 0, kt == CKT - 1)
                    ins.then_inc(unit_used, 1)
                    u += 1
                elif step == ("hidT",):
                    pe.wait_ge(hid_gelu, 1)
                    for kind in range(2):
                        for k in range(2):
                            o = (2 * kind + k) * 2 * NC
                            ins = pe.transpose(ps[:, 6, o:o + 2 * NC], hid[:, kind, k * P:(k + 1) * P],
                                               c_identf[0:2 * NC, 0:2 * NC])
                    ins.then_inc(hid_turned, 1)
                elif step == ("cmp2",):
                    pe.wait_ge(late_in, 16 * LATE)
                    pe.wait_ge(hid_out, 1)
                    for k in range(2):
                        pe.matmul(ps[0:2 * NC, 7, 0:HD], hidT[:, k, :], c_w2[:, 0, k, :], start=k == 0, stop=k == 1)
                    for k in range(2):
                        ins = pe.matmul(ps[:, 6, 0:HD], hidR[:, k, :, :].rearrange("p m n -> p (m n)"), c_w2[:, 1, k, :],
                                        start=k == 0, stop=k == 1)
                    ins.then_inc(cmp_ready, 1)
                elif step == ("kcT",):
                    pe.wait_ge(kc_rot, 1)
                    pe.transpose(ps[:, 7, 0:2 * NC], kcr[:, 0:2, :].rearrange("p k d -> p (k d)"), c_identf[0:2 * NC, 0:2 * NC]).then_inc(kc_turned, 1)
                elif step == ("cscore",):
                    pe.wait_ge(kc_out, 1)
                    pe.wait_ge(vc_out, 1)
                    pe.wait_ge(turned_out, 1)
                    for t in range(TT):
                        for i in range(NSA_PER):
                            for g in range(NSA_G):
                                rows = slice(g * HD, (g + 1) * HD)
                                o = (4 * t + i) * 16
                                ins = pe.matmul(ps[:, 6 + g, o:o + NC], qkT[rows, TQ + i, t * P:(t + 1) * P],
                                                kcT[rows, g * NC:(g + 1) * NC], start=True, stop=True)
                    ins.then_inc(cs_ready, 1)

            def it_qk(n):
                kind, j, t = ITEMS[n]
                o, w = s_half(n), P * (t + 1)
                tok = slice(t * P, (t + 1) * P)
                if n >= 2:
                    pe.wait_ge(it_exp, exps[n - 2])
                if kind == "dil":
                    for g in range(NG):
                        hd = g * SLOTS + j
                        rows = slice(HD * (hd % 2), HD * (hd % 2) + HD)
                        pe.matmul(psh[:, o + g, 0:w], qkT[rows, TDQ + hd // 2, tok], qkT[rows, TDK + hd // 2, 0:w],
                                  start=g != 1, stop=False, skip_group_check=True)
                    msk = c_mask[:, 0:NG, :] if t else c_mask[:, 0:NG, P:SEQ]
                    pe.matmul(psh[:, o:o + 2, 0:w], c_identb[:], msk[:, 0:2, :], start=False, stop=True,
                              skip_group_check=True)
                    pe.matmul(psh[:, o + 2, 0:w], c_identb[:], msk[:, 2, :], start=False, stop=True,
                              skip_group_check=True).then_inc(it_scores, 1)
                    return
                for g in range(NSA_G):
                    rows = slice(g * HD, (g + 1) * HD)
                    pe.matmul(psh[:, o + 2 * g:o + 2 * g + 2, 0:w], qkT[rows, TQ + j, tok],
                              qkT[rows, TSLC:TWIN + 1, 0:w], start=True, stop=False, skip_group_check=True)
                for g in range(NSA_G):
                    ins = pe.matmul(psh[:, o + 2 * g:o + 2 * g + 2, w - P:w], c_identb[:],
                                    c_mask[:, 0:1, P:SEQ].to_broadcast([P, 2, P]), start=False, stop=True,
                                    skip_group_check=True)
                ins.then_inc(it_scores, 1)

            def it_turn(n):
                t = ITEMS[n][2]
                w = P * (t + 1)
                pe.wait_ge(it_exp, exps[n])
                if n >= 1:
                    pe.wait_ge(it_pT0, n)
                if t and wide_before(n):
                    pe.wait_ge(it_pT1, wide_before(n))
                if n == PC_TURN + 1:
                    pe.wait_ge(pc_out, 1)
                elif n - 1 in PC_VALUES:
                    pe.wait_ge(oc_out, PC_VALUES.index(n - 1) + 1)
                blk = 0
                for m in range(maps_of(n)):
                    for k in range(t + 1):
                        ins = pe.transpose(psq[:, 16 + blk, :], probs[:, n % 2, m * w + k * P:m * w + (k + 1) * P],
                                           c_identf[:])
                        blk += 1
                ins.then_inc(it_turned, 1)

            def compressed_turn():
                pe.wait_ge(it_pT1, wide_before(PC_TURN))
                pe.wait_ge(cs_step, 9)
                pe.wait_ge(vc_zero, 2)
                for t in range(TT):
                    ins = pe.transpose(psq[:, 20 + t, :], pcm[:, CM * t:CM * (t + 1), :].rearrange("p m n -> p (m n)"),
                                       c_identf[:])
                ins.then_inc(pc_turned, 1)

            def compressed_values(n):
                pe.wait_ge(it_pT1, wide_before(n))
                pe.wait_ge(pc_out, 1)
                pe.matmul(ps[:, 5, :], pcT[:, PC_VALUES.index(n), :], vc[:].rearrange("p m d -> p (m d)"), start=True,
                          stop=True).then_inc(oc_ready, 1)

            def it_values(n):
                kind, j, t = ITEMS[n]
                s, bank = n % 2, 6 + n % 2
                pe.wait_ge(it_pT0, n + 1)
                if t:
                    pe.wait_ge(it_pT1, wide_before(n) + 1)
                if n >= 2:
                    pe.wait_ge(it_o, outs[n - 2])
                    if n - 2 in TURNS:
                        pe.wait_ge(ot_lo, turns_before(n - 2) + 1)
                maps = maps_of(n)
                for m in range(maps):
                    if kind == "dil":
                        v0, col = V_DIL + (m * SLOTS + j) * HD, 0
                    else:
                        v0, col = (V_SLC, V_WIN)[m % 2] + (m // 2) * HD, m * HD
                    for kt in range(t + 1):
                        k = m * (t + 1) + kt
                        ins = pe.matmul(ps[:, bank, col:col + HD], probsT[:, s, k * P:(k + 1) * P],
                                        vbuf[:, kt, v0:v0 + HD], start=k == 0, stop=k == maps * (t + 1) - 1,
                                        skip_group_check=True)
                ins.then_inc(it_pv, 1)

            def out_turn(n):
                tile, t = TILE_OF[n], ITEMS[n][2]
                pe.wait_ge(it_o, outs[n])
                pe.transpose(psq[:, 4 * (6 + n % 2) + 3, :], xn[:, t, tile * P:(tile + 1) * P],
                             c_identf[:]).then_inc(ot_turned, 1)

            exps = [sum(1 if ITEMS[k][0] == "dil" else 4 for k in range(n + 1)) for n in range(NI)]
            outs = [sum(1 if ITEMS[k][0] == "dil" else 2 for k in range(n + 1)) for n in range(NI)]
            pe.wait_ge(mask_cast, 1)
            pe.wait_ge(turned_out, 5)
            it_qk(0)
            pe.wait_ge(in_free_act, EVEN_ACT)
            for n in range(NI + 2):
                if n + 1 < NI:
                    it_qk(n + 1)
                if n < NI:
                    it_turn(n)
                if n == PC_TURN:
                    compressed_turn()
                elif n in PC_VALUES:
                    compressed_values(n)
                if n - 2 in TURNS:
                    out_turn(n - 2)
                if 1 <= n <= NI:
                    it_values(n - 1)
            pe.wait_ge(ot_lo, len(TURNS))
            out_proj("out0", 0, EVEN_KT, xhi, xlo)

            def ffn(layer):
                for t in range(TT):
                    pre(2 * layer + 1, t)
                pe.wait_ge(pre_lo, 2 * TT * (2 * layer + 2))
                u0, k0 = FIRST_UNIT[f"up{layer}"], layer * UP_CHUNKS

                def up_chunk(par, slots, at):
                    for half in range(2):
                        slot = slots[half]
                        pe.wait_ge(lo_done, at[half] + 1)
                        for m in range(4):
                            for b in range(4):
                                kt = 4 * half + b
                                cols = slice(b * BLK + m * P, b * BLK + (m + 1) * P)
                                ins = three(psh[:, 4 * par + m, :], whi[:, slot, cols], wlo[:, slot, cols],
                                            xhi[:, kt, :], xlo[:, kt, :], kt == 0 and m % 2 == 0, kt == KT - 1, True)
                        ins.then_inc(unit_used, 1)

                up_chunk(0, (u0 % RING, (u0 + 1) % RING), (u0, u0 + 1))
                with pe.Fori(0, (UP_CHUNKS - 1) // 2) as i:
                    for j in range(2):
                        v = u0 + 2 + 2 * j
                        if j == 1:
                            pe.wait_ge(up_free, 1 + k0 + 2 * i + 1)
                        else:
                            pe.wait_ge(up_free, 1 + k0 + 2 * i)
                        up_chunk((1 + j) % 2, (v % RING, (v + 1) % RING), (4 * i + v, 4 * i + v + 1))
                out_proj(f"down{layer}", 2 * layer + 1, FT, hid_hi, hid_lo,
                         lambda chunk: pe.wait_ge(up_lo, k0 + chunk + 1))

            ffn(0)

            pre(2, 0)
            u = FIRST_UNIT["in1"]
            for step in ODD_STEPS:
                if step[0] == "unit":
                    c, half = step[1:]
                    if c >= 2 and half == 0:
                        pe.wait_ge(in_free_act, EVEN_ACT + c - 1)
                    if c > 0:
                        in_unit(u, 2 * (c % 2), half)
                    elif half == 1:
                        first_units(u - 1, 2)
                    u += 1
                else:
                    c = step[1]
                    pe.wait_ge(in_free_act, EVEN_ACT + c + 1)
                    if c >= 2:
                        pe.wait_ge(turned_out, EVEN_ROT + c - 1)
                    for tile in range(4):
                        for t in range(TT):
                            ins = pe.transpose(psq[:, 16 + 8 * (c % 2) + 2 * tile + t, :],
                                               xn[:, c % 2, t * BLK + tile * P:t * BLK + (tile + 1) * P], c_identf[:])
                    ins.then_inc(turned, 1)

            def sb_scores(n):
                s = n % 3
                if n >= 3:
                    pe.wait_ge(sb_prob, n - 2)
                for hd in range(2):
                    rows, bank = slice(HD * hd, HD * hd + HD), 2 * s + hd
                    pe.matmul(ps[:, bank, 0:SEQ], qkT[rows, NP + n, 0:P], qkT[rows, n, :], start=True, stop=False,
                              skip_group_check=True)
                    pe.matmul(ps[:, bank, SEQ:SEQ + P], qkT[rows, NP + n, P:SEQ], qkT[rows, n, P:SEQ], start=False,
                              stop=False, skip_group_check=True)
                for hd in range(2):
                    diag = psq[:, 4 * (2 * s + hd):4 * (2 * s + hd) + 3:2, :]
                    ins = pe.matmul(diag, c_identb[:], c_mask[:, NG:NG + 1, 0:P].to_broadcast([P, 2, P]), start=False,
                                    stop=False, skip_group_check=True)
                ins.then_inc(sb_z, 1)

            def sb_sums(n):
                s = n % 3
                pe.wait_ge(sb_spd, n + 1)
                for hd in range(2):
                    bank = 2 * s + hd
                    pe.matmul(ps[:, bank, 0:384], c_tri[:, 0, :], sb_sp[:, n % 2, hd, :], start=False, stop=False,
                              skip_group_check=True)
                    ins = pe.matmul(ps[:, bank, P:SEQ], c_tri[:, 1, :], sb_sp[:, n % 2, hd, SEQ:SEQ + P], start=False,
                                    stop=True, skip_group_check=True)
                ins.then_inc(sb_cum, 1)

            def sb_values(n):
                pe.wait_ge(sb_prob, n + 1)
                if n >= 2:
                    pe.wait_ge(sb_olo, n - 1)
                for hd in range(2):
                    v0 = (2 * n + hd) * HD
                    o = ps[HD * hd:HD * hd + HD, 6 + n % 2, :]
                    pe.matmul(o[:, 0:SEQ], vbuf[:, 0, v0:v0 + HD], sb_a[:, n % 2, hd, 0:SEQ], start=True, stop=False)
                    ins = pe.matmul(o[:, P:SEQ], vbuf[:, 1, v0:v0 + HD], sb_a[:, n % 2, hd, SEQ:SEQ + P], start=False,
                                    stop=True)
                ins.then_inc(sb_pv, 1)

            pe.wait_ge(turned_out, EVEN_ROT + 4)
            pe.wait_ge(in_free_act, EVEN_ACT + 6)
            sb_scores(0)
            for n in range(NP + 1):
                if n + 1 < NP:
                    sb_scores(n + 1)
                if n < NP:
                    sb_sums(n)
                if n >= 1:
                    sb_values(n - 1)
            pe.wait_ge(sb_olo, NP)
            out_proj("out1", 2, KT, xhi, xlo)
            ffn(1)


def lay_out(x, norm_g, even_w_in, even_w_out, cmp_pe, cmp_w1, cmp_w2, odd_w_in, odd_w_out, ffn_w_up, ffn_conv_w,
            ffn_conv_b, ffn_w_down):
    f32 = np.float32

    def blocks_in(w):
        k, n = w.shape
        v = w.reshape(k // (4 * P), 4, P, n // BLK, BLK)
        return v.transpose(3, 0, 2, 1, 4).reshape(-1, P, UNIT)

    def blocks_out(w):
        k, n = w.shape
        v = w.reshape(k // P, P, n // BLK, BLK).transpose(2, 0, 1, 3).reshape(-1, 4, P, BLK)
        return v.transpose(0, 2, 1, 3).reshape(-1, P, UNIT)

    w = even_w_in[0]
    kv = NSA_HEADS * HD
    gate0 = kv + 2 * BRANCH * NSA_G * HD
    dil0 = gate0 + NSA_HEADS * BRANCH
    ndil = NG * SLOTS * HD
    pair = [e for i in range(NSA_PER) for e in (i, NSA_PER + i)]
    kvc = [w[:, kv + j * P:kv + (j + 1) * P] for j in range(2 * BRANCH)]
    q = w[:, :kv].reshape(D, NSA_HEADS, HD)[:, pair].reshape(D, kv)
    w_in0 = np.concatenate([kvc[0], kvc[1], kvc[3], kvc[5], q, w[:, dil0:dil0 + 2 * ndil], kvc[2], kvc[4],
                            w[:, dil0 + 2 * ndil:]], axis=1)
    in0 = blocks_in(w_in0)
    c1 = cmp_w1[0].reshape(2, 2, 8, P, CMP_H).transpose(0, 1, 3, 2, 4).reshape(4, P, UNIT)
    w_out0 = np.concatenate([even_w_out[0][:kv].reshape(NSA_HEADS, HD, D)[pair].reshape(kv, D), even_w_out[0][kv:]])

    def up(layer):
        v = ffn_w_up[layer].reshape(D, 2, UP_CHUNKS, 2 * P).transpose(0, 2, 1, 3).reshape(D, 2 * D_FF)
        return blocks_in(v)

    weights = np.concatenate([in0[:6], c1[:2], in0[6:8], c1[2:], in0[8:], blocks_out(w_out0), up(0),
                              blocks_out(ffn_w_down[0]), blocks_in(odd_w_in[0]), blocks_out(odd_w_out[0]), up(1),
                              blocks_out(ffn_w_down[1])])
    assert weights.shape == (NUNITS, P, UNIT)

    wgate = w[:, gate0:dil0].reshape(KT, P, NSA_HEADS * BRANCH).transpose(1, 0, 2)
    cmpw2 = cmp_w2[0].reshape(2, 2, P, HD).transpose(2, 0, 1, 3)
    pe2 = cmp_pe[0].reshape(2, CKT, 2, HD).transpose(2, 3, 0, 1).reshape(P, 2, CKT)
    gpre = norm_g[:, 0::2].reshape(4, D)
    gpost = norm_g[:, 1::2].reshape(4, D)
    taps = np.concatenate([ffn_conv_w, ffn_conv_b[:, None]], axis=1)
    convw = taps.reshape(2, 4, 2, UP_CHUNKS, 2, P).transpose(5, 0, 3, 2, 4, 1).reshape(P, -1)

    def rotary(pos):
        inv = np.power(f32(10000.0), -np.arange(HD // 2, dtype=f32) / f32(HD // 2)).astype(f32)
        ang = pos.astype(f32)[:, None] * inv[None, :]
        cos, sin = np.cos(ang), np.sin(ang)
        return np.stack([np.concatenate([cos, cos], 1), np.concatenate([-sin, sin], 1)])

    tab = rotary(np.arange(SEQ)).reshape(2, TT, P, HD).transpose(2, 0, 1, 3)
    rope = np.stack([tab * f32(SCALE), tab], axis=1)
    ends = np.arange(NC) * CMP_STRIDE + CMP_LEN - 1
    ropec = np.tile(rotary(ends), (1, 2, 1)).transpose(1, 0, 2)
    seen = ends[None, :] <= np.arange(SEQ)[:, None]
    cmask = np.stack([np.where(seen, 0.0, NEG), seen]).reshape(2, TT, P, NC).transpose(2, 0, 1, 3)
    t, k = P + np.arange(P)[:, None], np.arange(SEQ)[None, :]
    ok = [(k <= t) & (t - k <= win) & ((t - k) % dil == 0) for win, dil in zip(DIL_WINDOW, DIL)]
    ok.append(np.arange(P)[:, None] < np.arange(SEQ)[None, :])
    masks = np.where(np.stack(ok, 1), 0.0, NEG)
    tri = -np.stack([np.arange(P)[:, None] >= np.arange(P)[None, :], np.ones((P, P))], 1)
    blocks = np.arange(P)[:, None] // NCP == np.arange(CM)[None, :]
    arrays = dict(x=x.reshape(SEQ, D), weights=weights, wgate=wgate, cmpw2=cmpw2, pe2=pe2, gpre=gpre, gpost=gpost,
                  convw=convw, rope=rope.astype(f32), ropec=ropec.astype(f32), cmask=cmask.astype(f32), blocks=blocks.astype(f32),
                  masks=masks.astype(f32), identf=np.eye(P, dtype=f32),
                  tri=tri.astype(f32))
    return {n: np.ascontiguousarray(v) for n, v in arrays.items()}


def kernel(**inputs):
    import concourse.bacc as bacc
    from concourse.bass_utils import run_bass_kernel_spmd

    arrays = lay_out(**{n: np.asarray(v) for n, v in inputs.items()})
    nc = bacc.Bacc("TRN2", target_bir_lowering=False, num_devices=1)
    args = {n: nc.dram_tensor(f"in_{n}", v.shape, mybir.dt.from_np(v.dtype), kind="ExternalInput").ap()
            for n, v in arrays.items()}
    out = nc.dram_tensor("out_0", (SEQ, D), F32, kind="ExternalOutput").ap()
    build(nc, out=out, **args)
    r = run_bass_kernel_spmd(nc, [{f"in_{n}": v for n, v in arrays.items()}], core_ids=[0])
    return r.results[0]["out_0"].reshape(1, SEQ, D)
```

```python
from contextlib import ExitStack

import numpy as np

import concourse.bass as bass
from concourse import mybir

F32 = mybir.dt.float32
F32R = mybir.dt.float32r
BF16 = mybir.dt.bfloat16
U32 = mybir.dt.uint32
ALU = mybir.AluOpType
ACT = mybir.ActivationFunctionType
AX = mybir.AxisListType

P = 128
SEQ = 256
TT = SEQ // P
D = 1024
KT = D // P
HD = 64
EPS = 1e-6
NEG = -1e30

NSA_HEADS = 8
NSA_G = 2
NSA_PER = NSA_HEADS // NSA_G
BRANCH = 3
CMP_LEN = 32
CMP_STRIDE = 16
NC = (SEQ - CMP_LEN) // CMP_STRIDE + 1
NCP = 16
CM = P // NCP
CMP_H = 256
CKT = CMP_LEN * HD // P
DIL = (1, 4, 16)
DIL_WINDOW = (128, 512, 2048)
NG = len(DIL)
SLOTS = 4
D_FF = 2816
FT = D_FF // P
TAPS = 3
SB_HEADS = 16
SCALE = HD ** -0.5

BLK = 512
UNIT = 4 * BLK
RING = 4
LOOK = 2

UP_CHUNKS = 2 * FT * P // BLK
EVEN_KT = (NSA_HEADS + SLOTS) * HD // P
STAGES = [("in0", 7 * 2 + 4), ("out0", 2 * EVEN_KT // 4), ("up0", UP_CHUNKS * 2), ("down0", 2 * FT // 4),
          ("in1", 6 * 2), ("out1", 2 * KT // 4), ("up1", UP_CHUNKS * 2), ("down1", 2 * FT // 4)]
FIRST_UNIT = {}
NUNITS = 0
for _name, _n in STAGES:
    FIRST_UNIT[_name] = NUNITS
    NUNITS += _n

TQ, TDQ, TDK, TSLC, TWIN = 0, 4, 10, 16, 17
V_KC, V_VC, V_SLC, V_WIN, V_DIL = 0, 128, 256, 384, 512
TABLES, LATE = 3, 6


def build(nc, x, weights, wgate, cmpw2, pe2, gpre, gpost, convw, rope, ropec, cmask, blocks, masks, identf, tri,
          out):
    ctx = ExitStack()
    with ctx:
        def sem(name):
            return ctx.enter_context(nc.semaphore(name))

        def sb(name, shape, dt=F32, c=ctx):
            return c.enter_context(nc.sbuf_tensor(name, shape, dt))

        h = sb("h", [P, TT, D])
        xn = sb("xn", [P, TT, D])
        xhi = sb("xhi", [P, KT, SEQ], F32R)
        xlo = sb("xlo", [P, KT, SEQ], F32R)
        raw = sb("raw", [P, RING, UNIT])
        whi = sb("whi", [P, RING, UNIT], F32R)
        wlo = sb("wlo", [P, RING, UNIT], F32R)
        c_gpre = sb("c_gpre", [P, D])
        c_gpost = sb("c_gpost", [P, D])
        c_conv = sb("c_conv", [P, 2 * UP_CHUNKS * 4 * 4])
        c_rope = sb("c_rope", [P, 2, 2, TT, HD])
        c_ropec = sb("c_ropec", [2 * NC, 2, HD])
        c_cmask = sb("c_cmask", [P, 2, TT, NC])
        c_mask = sb("c_mask", [P, NG + 1, SEQ], BF16)
        c_identf = sb("c_identf", [P, P])
        c_identb = sb("c_identb", [P, P], BF16)
        c_tri = sb("c_tri", [P, 2, P])
        c_wg = sb("c_wg", [P, KT, NSA_HEADS * BRANCH])
        wg_parts = sb("wg_parts", [P, 2, KT, NSA_HEADS * BRANCH], F32R)
        wg_hi, wg_lo = wg_parts[:, 0], wg_parts[:, 1]
        tri_r = wg_parts[:].rearrange("p a k n -> p (a k n)")[:, 0:2 * P].rearrange("p (a c) -> p a c", a=2)
        c_w2 = sb("c_w2", [P, 2, 2, HD])
        c_pe2 = sb("c_pe2", [P, 2, CKT])
        meanh = sb("meanh", [P, 2, TT, 2])
        ms = sb("ms", [P, 2, TT])
        rstd = sb("rstd", [P, 2, TT])
        mhalf = sb("mhalf", [P, 1])

        a = ctx.enter_context(ExitStack())
        vbuf = sb("vbuf", [P, TT, 1280], F32, a)
        qkT = sb("qkT", [P, 18, SEQ], F32, a)
        gates = sb("gates", [P, TT, NSA_HEADS * BRANCH], F32, a)
        kcT = sb("kcT", [P, 2, NCP], F32, a)
        vc = sb("vc", [P, CM, HD], F32, a)
        stat = sb("stat", [P, 4, 8], F32, a)
        coef = sb("coef", [P, 2, 8], F32, a)
        stc = sb("stc", [P, 3, TT * CM], F32, a)
        pcm = sb("pcm", [P, TT * CM, NCP], F32, a)
        pcT = sb("pcT", [P, TT, P], F32, a)
        blockd = sb("c_blockd", [P, CM], F32, a)
        b = a.enter_context(ExitStack())
        t12 = sb("t12", [P, 2, TT, BLK], F32, b)
        mask_f = t12[:, 0, :, :].rearrange("p t (m c) -> p (t m) c", c=SEQ)
        x2 = sb("x2", [P, 4, P], F32, b)
        gatesT = x2[0:NSA_HEADS * BRANCH, 0:2, :].rearrange("p k c -> p (k c)")
        xbf = sb("xbf", [P, 2, CKT * 2 * NC], F32, b)
        xb_hi = sb("xb_hi", [P, 2, CKT * 2 * NC + P], F32R, b)
        xb_lo = sb("xb_lo", [P, 2, CKT * 2 * NC + P], F32R, b)
        hid = sb("hid", [2 * NC, 2, CMP_H], F32, b)
        hidT = sb("hidT", [P, 2, 2 * NC], F32, b)
        hidR = sb("hidR", [P, 2, CM, NCP], F32, b)
        kcr = sb("kcr", [2 * NC, 4, HD], F32, b)
        b.close()
        b = a.enter_context(ExitStack())
        probs = sb("probs", [P, 2, 1024], F32, b)
        probsT = sb("probsT", [P, 2, 1024], F32, b)
        b.close()
        sb_sp = sb("sb_sp", [P, 3, 2, 384], F32, b)
        sb_sphi = sb("sb_sphi", [P, 2, 2, 384], F32R, b)
        sb_splo = sb("sb_splo", [P, 2, 2, 384], F32R, b)
        sb_a = sb("sb_a", [P, 2, 2, 384], F32, b)
        b.close()
        a.close()
        hid_hi = sb("hid_hi", [P, FT, SEQ], F32R, a)
        hid_lo = sb("hid_lo", [P, FT, SEQ], F32R, a)
        conv = sb("conv", [P, 2, 4, SEQ], F32, a)
        act_g = sb("act_g", [P, 2, 2, SEQ], F32, a)
        hidf = sb("hidf", [P, 2, 2, SEQ], F32, a)

        ps = ctx.enter_context(nc.psum_tensor("ps", [P, 8, BLK], F32))
        psq = ps[:, :, :].rearrange("p b (q c) -> p (b q) c", c=P)
        psh = ps[:, :, :].rearrange("p b (q c) -> p (b q) c", c=SEQ)

        ident_in, gpre_in, gpost_in, wg_in, tables_in, late_in = (
            sem(s + "_in") for s in ("ident", "gpre", "gpost", "wg", "tables", "late"))
        x_in = [sem(f"x_in{t}") for t in range(TT)]
        out_done = sem("out_done")
        raw_in = [sem(f"raw_in{s}") for s in range(RING)]
        first_in = [sem(f"first_in{i}") for i in range(4)]
        first_hi, first_lo = sem("first_hi"), sem("first_lo")
        hi_done, lo_done, unit_used = sem("hi_done"), sem("lo_done"), sem("unit_used")
        half_set, mask_cast = sem("half_set"), sem("mask_cast")
        pre_sq, pre_ms, pre_rstd, pre_xn, pre_tr, pre_hi, pre_lo = (
            sem("pre_" + s) for s in ("sq", "ms", "rstd", "xn", "tr", "hi", "lo"))
        y_done = [sem(f"y_done{t}") for t in range(TT)]
        post_sq, post_ms, post_rstd, post_yg, post_h = (
            sem(s) for s in ("post_sq", "post_ms", "post_rstd", "post_yg", "post_h"))
        in_free_act = sem("in_free_act")
        rope_parts, staged, turned, turned_out = sem("rope_parts"), sem("staged"), sem("turned"), sem("turned_out")
        wg_done, gate_ready, gate_tanh, gate_turned, gate_done = (
            sem(s) for s in ("wg_done", "gate_ready", "gate_tanh", "gate_turned", "gate_done"))
        x2_turned, x2_out, xb_pad, xb_sum, xb_hid, xb_split = (
            sem(s) for s in ("x2_turned", "x2_out", "xb_pad", "xb_sum", "xb_hid", "xb_split"))
        hid_gelu, hid_turned, hid_out = (sem(s) for s in ("hid_gelu", "hid_turned", "hid_out"))
        cmp_ready, kc_prod, kc_rot, vc_out, kc_turned, kc_out = (
            sem(s) for s in ("cmp_ready", "kc_prod", "kc_rot", "vc_out", "kc_turned", "kc_out"))
        cs_ready, cs_step, cs_exp, pc_turned, pc_out, oc_ready, oc_out = (
            sem(s) for s in ("cs_ready", "cs_step", "cs_exp", "pc_turned", "pc_out", "oc_ready", "oc_out"))
        vc_zero, kc_zero = sem("vc_zero"), sem("kc_zero")
        it_scores, it_max, it_exp, it_coef, it_turned, it_pT0, it_pT1, it_pv, it_o, ot_turned, ot_hi, ot_lo = (
            sem("it_" + s) for s in ("scores", "max", "exp", "coef", "turned", "pT0", "pT1", "pv", "o", "ot_turned",
                                     "ot_hi", "ot_lo"))
        tri_cast = sem("tri_cast")
        sb_z, sb_absd, sb_exp1, sb_ln, sb_spd, sb_sph, sb_spl, sb_cum, sb_prob, sb_pv, sb_ohi, sb_olo = (
            sem("sb_" + s) for s in ("z", "absd", "exp1", "ln", "spd", "sph", "spl", "cum", "prob", "pv", "ohi", "olo"))
        up_tok, up_staged, up_turned, up_ident, up_tap1, up_free, up_gelu, up_hf, up_hi, up_lo = (
            sem("up_" + s) for s in ("tok", "staged", "turned", "ident", "tap1", "free", "gelu", "hf", "hi", "lo"))

        EVEN_STEPS = [("unit", 0, 0), ("unit", 0, 1), ("gate",), ("unit", 1, 0), ("gateT",), ("x2T",), ("unit", 1, 1),
                      ("unit", 2, 0), ("turn", 1), ("unit", 2, 1), ("cmp1", 0, 0), ("cmp1", 0, 1),
                      ("unit", 3, 0), ("turn", 2), ("unit", 3, 1), ("cmp1", 1, 0), ("cmp1", 1, 1),
                      ("unit", 4, 0), ("turn", 3), ("hidT",), ("unit", 4, 1), ("cmp2",), ("unit", 5, 0),
                      ("turn", 4), ("kcT",), ("unit", 5, 1), ("cscore",), ("unit", 6, 0), ("turn", 5),
                      ("unit", 6, 1)]
        ODD_STEPS = [("unit", c, half) for c in range(6) for half in range(2)]
        ODD_TILE = {1: 0, 2: SB_HEADS // 2, 3: 4, 4: SB_HEADS // 2 + 4}
        EVEN_ACT = 3
        EVEN_ROT = 5

        ITEMS = [("dil", j, t) for j in range(SLOTS) for t in range(TT)] + \
                [("nsa", i, t) for i in range(NSA_PER) for t in range(TT)]
        NI = len(ITEMS)
        TURNS = [n for n, (kind, j, t) in enumerate(ITEMS) if t == TT - 1 and (kind == "nsa" or j % 2)]
        PC_TURN, PC_VALUES = 2, (4, 6)
        SPLIT_AT = (14, 15, 16, 17)
        NP = SB_HEADS // 2

        def sb_bank(n):
            return 2 * ((n + 2) % 3)

        def s_half(n):
            return 4 * ((n + 1) % 2)

        NSA0 = SLOTS // 2
        TILE_OF = [j // 2 if kind == "dil" else NSA0 + j for kind, j, _ in ITEMS]

        def turns_before(n):
            return sum(1 for m in TURNS if m < n)

        def wide_before(n):
            return sum(1 for m in range(n) if ITEMS[m][2])

        def ends(steps, first):
            u, found = first, {}
            for step in steps:
                if step[0] in ("unit", "cmp1"):
                    u += 1
                    if step[2] == 1:
                        found[step[:2]] = u
            return found

        EVEN_END, ODD_END = ends(EVEN_STEPS, FIRST_UNIT["in0"]), ends(ODD_STEPS, FIRST_UNIT["in1"])
        TILE_MAJOR = [(c, t) for t in range(TT) for c in range(2)]
        HALF_MAJOR = [(c, t) for c in range(2) for t in range(TT)]
        Y_ORDER = [TILE_MAJOR, HALF_MAJOR, HALF_MAJOR, HALF_MAJOR]
        Y_BANK = (0, 4, 2, 4)
        T_BANK = (4, 4, 0, 0)
        UP_BANK = (4, 6)

        HALVED = 2

        def uhalf(i):
            return slice(i * UNIT // 2, (i + 1) * UNIT // 2)

        def colhalf(c):
            return slice(c * BLK, (c + 1) * BLK)

        def maps_of(n):
            return NG if ITEMS[n][0] == "dil" else 4

        block = ctx.enter_context(nc.Block())

        @block.sync
        def _(sp):
            sp.dma_start(h[:, 0, :], x[0:P, :]).then_inc(x_in[0], 16)
            for u in range(HALVED):
                for i in range(2):
                    sp.dma_start(raw[:, u, uhalf(i)], weights[u, :, uhalf(i)]).then_inc(first_in[2 * u + i], 16)
            sp.dma_start(h[:, 1, :], x[P:2 * P, :]).then_inc(x_in[1], 16)
            for u in range(HALVED, RING):
                sp.dma_start(raw[:, u, :], weights[u]).then_inc(raw_in[u], 16)
            for signal, dst, src in ((wg_in, c_wg[:], wgate), (tables_in, mask_f, masks), (tables_in, c_rope[:], rope),
                                     (tables_in, c_pe2[:], pe2), (late_in, c_w2[:], cmpw2),
                                     (late_in, c_ropec[:], ropec), (late_in, c_cmask[:], cmask),
                                     (late_in, blockd[:], blocks), (late_in, c_tri[:], tri), (late_in, c_conv[:], convw)):
                sp.dma_start(dst, src).then_inc(signal, 16)
            rounds = (NUNITS - RING) // RING
            with sp.Fori(0, rounds) as i:
                for s in range(RING):
                    sp.wait_ge(lo_done, RING * i + (s + 1))
                    sp.dma_start(raw[:, s, :], weights[bass.ds(RING * i + (RING + s), 1)]
                                 .rearrange("u p n -> (u p) n")).then_inc(raw_in[s], 16)
            for u in range(RING + rounds * RING, NUNITS):
                sp.wait_ge(lo_done, u - RING + 1)
                sp.dma_start(raw[:, u % RING, :], weights[u]).then_inc(raw_in[u % RING], 16)
            for t in range(TT):
                for c in range(2):
                    sp.wait_ge(post_h, 2 * (3 * TT + t) + c + 1)
                    sp.dma_start(out[t * P:(t + 1) * P, colhalf(c)], h[:, t, colhalf(c)]).then_inc(out_done, 16)
            sp.wait_ge(out_done, 16 * 2 * TT)

        @block.scalar
        def _(act):
            def load_gain(dst, src, p, signal):
                act.dma_start(dst[:], src[p:p + 1, :].partition_broadcast(P)
                              .rearrange("p a n -> p (a n)")).then_inc(signal, 16)

            load_gain(c_gpre, gpre, 0, gpre_in)
            act.dma_start(c_identf[:], identf).then_inc(ident_in, 16)
            act.preload_act_table_set("gelu_apprx_tanh_and_others")

            def split(slot, at, wait_used):
                act.wait_ge(raw_in[slot], 16 * (at[1] - (1 if slot < HALVED else 0)))
                if wait_used:
                    act.wait_ge(unit_used, at[0] - (RING - 1))
                act.copy(whi[:, slot, :], raw[:, slot, :]).then_inc(hi_done, 1)

            def split_half(u, i):
                slot = u % RING
                if u < HALVED:
                    act.wait_ge(first_in[2 * u + i], 16)
                elif i == 0:
                    act.wait_ge(raw_in[slot], 16 * (u // RING + 1 - (1 if slot < HALVED else 0)))
                    act.wait_ge(unit_used, u - (RING - 1))
                act.copy(whi[:, slot, uhalf(i)], raw[:, slot, uhalf(i)]).then_inc(hi_done if i else first_hi, 1)

            def split_ahead(u):
                v = u + LOOK
                if v < NUNITS:
                    split(v % RING, (v, v // RING + 1), v >= RING)

            def squares(p, t):
                for c in range(2):
                    if p == 0:
                        act.wait_ge(x_in[t], 16)
                    else:
                        act.wait_ge(post_h, 2 * ((p - 1) * TT + t) + c + 1)
                    act.activation(xn[:, t, colhalf(c)], h[:, t, colhalf(c)], ACT.Square, scale=D ** -0.5,
                                   accum_out=meanh[:, 0, t, c:c + 1]).then_inc(pre_sq, 1)

            def pre(p):
                squares(p, 0)
                post_squares(p - 1, 1)
                pre_his(p, 0)
                squares(p, 1)
                pre_his(p, 1)
                if p < 3:
                    next_gpre(p)
                load_gain(c_gpost, gpost, p, gpost_in)

            def next_gpre(p):
                act.wait_ge(pre_xn, 2 * TT * (p + 1))
                load_gain(c_gpre, gpre, p + 1, gpre_in)

            def pre_his(p, t):
                for c in range(2):
                    act.wait_ge(pre_tr, 2 * (p * TT + t) + c + 1)
                    act.copy(xhi[:, 4 * c:4 * c + 4, t * P:(t + 1) * P],
                             ps[:, T_BANK[p] + 2 * t + c, :].rearrange("p (k c) -> p k c", c=P)).then_inc(pre_hi, 1)

            def post_squares(p, part):
                order = Y_ORDER[p]
                cut = 2 if p == 0 else 3
                for c, t in order[:cut] if part == 0 else order[cut:]:
                    act.wait_ge(y_done[t], 2 * p + c + 1)
                    act.activation(xn[:, t, colhalf(c)], ps[:, Y_BANK[p] + 2 * t + c, :], ACT.Square,
                                   scale=D ** -0.5, accum_out=meanh[:, 1, t, c:c + 1]).then_inc(post_sq, 1)

            def plain_stage(name, ahead=0):
                for u in range(FIRST_UNIT[name] + ahead, FIRST_UNIT[name] + dict(STAGES)[name]):
                    split_ahead(u)

            squares(0, 0)
            split_half(0, 0)
            pre_his(0, 0)
            split_half(0, 1)
            split_half(1, 0)
            split_half(1, 1)
            squares(0, 1)
            pre_his(0, 1)
            next_gpre(0)
            load_gain(c_gpost, gpost, 0, gpost_in)

            def it_probs(n):
                kind, _, t = ITEMS[n]
                s, w, o, v = n % 2, P * (t + 1), s_half(n), n % 4
                act.wait_ge(it_max, n + 1)
                if n >= 2:
                    act.wait_ge(it_turned, n - 1)
                if kind == "dil":
                    act.activation(probs[:, s, 0:NG * w].rearrange("p (m c) -> p m c", c=w),
                                   psh[:, o:o + NG, 0:w], ACT.Exp, bias=stat[:, v, 0:1],
                                   accum_out=stat[:, v, 4:5]).then_inc(it_exp, 1)
                else:
                    for m in range(4):
                        act.activation(probs[:, s, m * w:(m + 1) * w], psh[:, o + m, 0:w], ACT.Exp,
                                       bias=stat[:, v, m:m + 1], accum_out=stat[:, v, 4 + m:5 + m]).then_inc(it_exp, 1)

            def it_turned_out(n):
                k = min(BLK, maps_of(n) * (ITEMS[n][2] + 1) * P)
                act.wait_ge(it_turned, n + 1)
                if n >= 2:
                    act.wait_ge(it_pv, n - 1)
                act.copy(probsT[:, n % 2, 0:k], ps[:, 4, 0:k]).then_inc(it_pT0, 1)

            def it_hi(n):
                act.wait_ge(ot_turned, turns_before(n) + 1)
                act.copy(xhi[:, TILE_OF[n], :], ps[:, 6 + n % 2, SEQ:2 * SEQ]).then_inc(ot_hi, 1)

            u = FIRST_UNIT["in0"]
            for step in EVEN_STEPS:
                if step[0] in ("unit", "cmp1"):
                    split_ahead(u)
                    u += 1
                if step == ("unit", 0, 0):
                    act.wait_ge(wg_in, 16)
                    act.copy(wg_hi[:], c_wg[:]).then_inc(wg_done, 1)
                elif step == ("unit", 0, 1):
                    act.wait_ge(unit_used, EVEN_END["unit", 0])
                    for t in range(TT):
                        src = ps[:, t, 0:4 * HD].rearrange("p (k d) -> p k d", d=HD).unsqueeze(2)
                        act.copy(xn[:, 0, t * BLK:(t + 1) * BLK].rearrange("p (k e d) -> p k e d", e=2, d=HD),
                                 src.to_broadcast([P, 4, 2, HD]))
                    act.copy(vbuf[:, :, V_SLC:BLK], ps[:, 0:2, V_SLC:BLK]).then_inc(in_free_act, 1)
                elif step == ("gate",):
                    act.wait_ge(gate_ready, 1)
                    act.activation(gatesT, ps[0:NSA_HEADS * BRANCH, 7, 0:SEQ], ACT.Tanh,
                                   scale=0.5).then_inc(gate_tanh, 1)
                elif step == ("x2T",):
                    act.wait_ge(x2_turned, 1)
                    for par in range(2):
                        v = psh[par * HD:(par + 1) * HD, 12:16, :].rearrange("p k (m two) -> p k m two", two=2)
                        act.copy(x2[par * HD:(par + 1) * HD, :, :], v[:, :, :, par]).then_inc(x2_out, 1)
                    act.wait_ge(xb_sum, 4)
                    act.copy(xb_hi[:, :, 0:CKT * 2 * NC], xbf[:]).then_inc(xb_hid, 1)
                elif step[0] == "turn":
                    c = step[1]
                    n = 2 if c == 5 else 4
                    act.wait_ge(turned, c)
                    act.copy(qkT[:, 4 * (c - 1):4 * (c - 1) + n, :], psh[:, 8:8 + n, :]).then_inc(turned_out, 1)
                elif step == ("cmp1", 1, 1):
                    act.wait_ge(unit_used, EVEN_END["cmp1", 1])
                    act.activation(hid[:], ps[0:2 * NC, 6:8, 0:CMP_H], ACT.Gelu_apprx_tanh).then_inc(hid_gelu, 1)
                elif step == ("unit", 5, 1):
                    act.wait_ge(unit_used, EVEN_END["unit", 5])
                    act.wait_ge(rope_parts, TT * 5)
                    act.copy(vbuf[:, :, 512:768], ps[:, 2:4, 256:512]).then_inc(in_free_act, 1)
                elif step == ("unit", 6, 1):
                    act.wait_ge(cs_step, 4)
                    act.activation(pcm[:, :, 0:NC], pcm[:, :, 0:NC], ACT.Exp).then_inc(cs_exp, 1)
                    it_probs(0)
                    it_probs(1)
                    act.wait_ge(unit_used, EVEN_END["unit", 6])
                    act.copy(vbuf[:, :, 768:1280], ps[:, 6:8, :]).then_inc(in_free_act, 1)

            for n in range(NI + 2):
                if n < NI:
                    it_turned_out(n)
                if n - 2 in TURNS:
                    it_hi(n - 2)
                if n + 2 < NI:
                    it_probs(n + 2)
                if n in SPLIT_AT:
                    k = SPLIT_AT.index(n)
                    split_half(FIRST_UNIT["out0"] + LOOK + k // 2, k % 2)
            plain_stage("out0", 2)
            post_squares(0, 0)

            def ffn(layer):
                pre(2 * layer + 1)
                act.wait_ge(late_in, 16 * LATE)
                act.preload_act_table_set("gelu_apprx_tanh_and_others")
                u0, k0 = FIRST_UNIT[f"up{layer}"], layer * UP_CHUNKS

                def identities(par, at, cofs):
                    act.wait_ge(unit_used, u0 + 2 + 2 * at)
                    for bank in range(2):
                        for m in (2 * bank, 2 * bank + 1):
                            act.activation(conv[:, par, m, :], psh[:, 4 * par + m, :], ACT.Identity,
                                           scale=c_conv[:, bass.ds(cofs + (4 * m + 2), 1)],
                                           bias=c_conv[:, bass.ds(cofs + (4 * m + 3), 1)]).then_inc(up_ident, 1)

                def gelu(par, at):
                    act.wait_ge(up_free, 1 + k0 + 1 + at)
                    act.activation(act_g[:, par], conv[:, par, 0:2, :], ACT.Gelu_apprx_tanh).then_inc(up_gelu, 1)

                def hidden_hi(par, at, tile):
                    act.wait_ge(up_hf, 1 + k0 + 1 + at)
                    act.copy(hid_hi[:, tile, :], hidf[:, par]).then_inc(up_hi, 1)

                split_ahead(u0)
                act.wait_ge(up_tok, layer + 1)
                act.copy(xn[:, 0, 0:BLK], ps[:, UP_BANK[layer], :]).then_inc(up_staged, 1)
                split_ahead(u0 + 1)
                act.wait_ge(unit_used, u0 + 2)
                act.copy(xn[:, 1, 0:BLK], ps[:, UP_BANK[layer] + 1, :]).then_inc(up_staged, 1)
                act.wait_ge(up_turned, layer + 1)
                identities(0, 0, layer * UP_CHUNKS * 16)
                with act.Fori(0, (UP_CHUNKS - 1) // 2) as i:
                    for j in range(2):
                        par = (1 + j) % 2
                        for half in range(2):
                            v = u0 + 2 + 2 * j + half + LOOK
                            split(v % RING, (4 * i + v, i + (v // RING + 1)), True)
                        gelu(1 - par, 2 * i + j)
                        if j == 0:
                            act.wait_ge(up_hf, 1 + k0 + 2 * i)
                        else:
                            act.wait_ge(up_hf, 1 + k0 + 2 * i + 1)
                        identities(par, 2 * i + (1 + j), (2 * i + (1 + j)) * 16 + layer * UP_CHUNKS * 16)
                        hidden_hi(1 - par, 2 * i + j, bass.ds(4 * i + 2 * j, 2))
                last = UP_CHUNKS - 1
                split_ahead(FIRST_UNIT[f"down{layer}"])
                gelu(last % 2, last)
                hidden_hi(last % 2, last, slice(2 * last, 2 * last + 2))
                plain_stage(f"down{layer}", 1)
                post_squares(2 * layer + 1, 0)

            ffn(0)

            def sb_soft(n):
                s = n % 3
                act.wait_ge(sb_absd, n + 1)
                act.activation(sb_sp[:, s], sb_sp[:, s], ACT.Exp).then_inc(sb_exp1, 1)
                act.wait_ge(sb_exp1, n + 1)
                act.activation(sb_sp[:, s], sb_sp[:, s], ACT.Ln, bias=1.0).then_inc(sb_ln, 1)

            def sb_soft_hi(n):
                act.wait_ge(sb_spd, n + 1)
                if n >= 2:
                    act.wait_ge(sb_cum, n - 1)
                act.copy(sb_sphi[:, n % 2], sb_sp[:, n % 3]).then_inc(sb_sph, 1)

            def sb_weights(n):
                act.wait_ge(sb_cum, n + 1)
                if n >= 2:
                    act.wait_ge(sb_pv, n - 1)
                act.activation(sb_a[:, n % 2], ps[:, sb_bank(n):sb_bank(n) + 2, 0:384], ACT.Exp).then_inc(sb_prob, 1)

            def sb_hi(n):
                act.wait_ge(sb_pv, n + 1)
                act.copy(xhi[:, n, :], ps[:, 6 + n % 2, 0:SEQ]).then_inc(sb_ohi, 1)

            pre(2)
            u = FIRST_UNIT["in1"]
            for step in ODD_STEPS:
                if step[0] == "unit":
                    split_ahead(u)
                    u += 1
                    if step == ("unit", 5, 0):
                        act.preload_act_table_set("natural_log_exp_and_others")
                        sb_soft(0)
                    if step[2] == 1:
                        c = step[1]
                        if c == 5:
                            sb_soft(1)
                            sb_soft_hi(0)
                        if c in (0, 5):
                            act.wait_ge(unit_used, ODD_END["unit", c])
                            act.copy(vbuf[:, :, (c // 5) * BLK:(c // 5 + 1) * BLK],
                                     ps[:, 2 * (c % 2):2 * (c % 2) + 2, :]).then_inc(in_free_act, 1)

            for n in range(NP + 1):
                if n < NP:
                    sb_weights(n)
                if n + 1 < NP:
                    sb_soft_hi(n + 1)
                if n + 2 < NP:
                    sb_soft(n + 2)
                if n >= 1:
                    sb_hi(n - 1)
            plain_stage("out1")
            post_squares(2, 0)
            ffn(1)
            post_squares(3, 1)

        @block.vector
        def _(dve):
            def split(slot, at):
                dve.wait_ge(hi_done, at + 1)
                dve.tensor_tensor(wlo[:, slot, :], raw[:, slot, :], whi[:, slot, :].bitcast(F32),
                                  ALU.subtract).then_inc(lo_done, 1)

            def split_half(u, i):
                slot = u % RING
                before = u if u < HALVED else HALVED + u - (FIRST_UNIT["out0"] + LOOK)
                if i == 0:
                    dve.wait_ge(first_hi, before + 1)
                else:
                    dve.wait_ge(hi_done, u + 1)
                    dve.wait_ge(first_lo, before + 1)
                dve.tensor_tensor(wlo[:, slot, uhalf(i)], raw[:, slot, uhalf(i)], whi[:, slot, uhalf(i)].bitcast(F32),
                                  ALU.subtract).then_inc(lo_done if i else first_lo, 1)

            def split_ahead(u):
                v = u + LOOK
                if v < NUNITS:
                    split(v % RING, v)

            def pre_ms_of(p, t):
                dve.wait_ge(pre_sq, 2 * (p * TT + t + 1))
                dve.tensor_scalar(ms[:, 0, t:t + 1], meanh[:, 0, t, 0:1], meanh[:, 0, t, 1:2], EPS, ALU.add,
                                  ALU.add).then_inc(pre_ms, 1)

            def pre_normed(p, t):
                dve.wait_ge(gpre_in, 16 * (p + 1))
                dve.wait_ge(pre_rstd, p * TT + t + 1)
                for c in range(2):
                    dve.scalar_tensor_tensor(xn[:, t, colhalf(c)], h[:, t, colhalf(c)], rstd[:, 0, t:t + 1],
                                             c_gpre[:, colhalf(c)], ALU.mult, ALU.mult).then_inc(pre_xn, 1)

            def pre_los(p, t):
                tok = slice(t * P, (t + 1) * P)
                for c in range(2):
                    dve.wait_ge(pre_hi, 2 * (p * TT + t) + c + 1)
                    dve.tensor_tensor(xlo[:, 4 * c:4 * c + 4, tok],
                                      ps[:, T_BANK[p] + 2 * t + c, :].rearrange("p (k c) -> p k c", c=P),
                                      xhi[:, 4 * c:4 * c + 4, tok].bitcast(F32), ALU.subtract).then_inc(pre_lo, 1)

            def post_gain(p, c, t):
                dve.wait_ge(post_sq, 4 * p + Y_ORDER[p].index((c, t)) + 1)
                dve.tensor_tensor(xn[:, t, colhalf(c)], ps[:, Y_BANK[p] + 2 * t + c, :], c_gpost[:, colhalf(c)],
                                  ALU.mult).then_inc(post_yg, 1)

            def post_ms_of(p, t):
                dve.wait_ge(post_sq, 4 * p + Y_ORDER[p].index((1, t)) + 1)
                dve.tensor_scalar(ms[:, 1, t:t + 1], meanh[:, 1, t, 0:1], meanh[:, 1, t, 1:2], EPS, ALU.add,
                                  ALU.add).then_inc(post_ms, 1)

            def post_residual(p, t):
                dve.wait_ge(post_yg, 2 * TT * p + (2 * t + 2 if Y_ORDER[p] is TILE_MAJOR else TT + t + 1))
                dve.wait_ge(post_rstd, TT * p + t + 1)
                for c in range(2):
                    dve.scalar_tensor_tensor(h[:, t, colhalf(c)], xn[:, t, colhalf(c)], rstd[:, 1, t:t + 1],
                                             h[:, t, colhalf(c)], ALU.mult, ALU.add).then_inc(post_h, 1)

            def junction(p):
                dve.wait_ge(gpost_in, 16 * (p + 1))
                post_gain(p, 0, 0)
                if Y_ORDER[p] is HALF_MAJOR:
                    post_gain(p, 0, 1)
                post_ms_of(p, 0)
                post_gain(p, 1, 0)
                post_residual(p, 0)
                if p < 3:
                    pre_ms_of(p + 1, 0)
                    pre_normed(p + 1, 0)
                if Y_ORDER[p] is TILE_MAJOR:
                    post_gain(p, 0, 1)
                post_ms_of(p, 1)
                post_gain(p, 1, 1)
                if p < 3:
                    pre_los(p + 1, 0)
                post_residual(p, 1)
                if p < 3:
                    pre_ms_of(p + 1, 1)
                    pre_normed(p + 1, 1)
                    pre_los(p + 1, 1)

            pre_ms_of(0, 0)
            pre_normed(0, 0)
            split_half(0, 0)
            pre_los(0, 0)
            split_half(0, 1)
            split_half(1, 0)
            split_half(1, 1)
            pre_ms_of(0, 1)
            pre_normed(0, 1)
            pre_los(0, 1)

            def rotate(c):
                bank = 2 * (c % 2)
                dve.wait_ge(unit_used, EVEN_END["unit", c])
                if c >= 2:
                    dve.wait_ge(staged, TT * (c - 1))
                parts = {1: [(0, 8, 0)], 2: [(0, 8, 0)], 3: [(0, 4, 0), (4, 8, 1)], 4: [(0, 8, 1)], 5: [(0, 4, 1)]}[c]
                for t in range(TT):
                    src = ps[:, bank + t, :].rearrange("p (h d) -> p h d", d=HD)
                    t1 = t12[:, 0, t, :].rearrange("p (h d) -> p h d", d=HD)
                    t2 = t12[:, 1, t, :].rearrange("p (h d) -> p h d", d=HD)
                    half = HD // 2
                    for lo, hi, which in parts:
                        n = hi - lo
                        cos = c_rope[:, which, 0, t, :].unsqueeze(1).to_broadcast([P, n, HD])
                        sin = c_rope[:, which, 1, t, :].unsqueeze(1)
                        dve.tensor_tensor(t1[:, lo:hi, :], src[:, lo:hi, :], cos, ALU.mult)
                        dve.tensor_tensor(t2[:, lo:hi, 0:half], src[:, lo:hi, half:HD],
                                          sin[:, :, 0:half].to_broadcast([P, n, half]), ALU.mult)
                        ins = dve.tensor_tensor(t2[:, lo:hi, half:HD], src[:, lo:hi, 0:half],
                                                sin[:, :, half:HD].to_broadcast([P, n, half]), ALU.mult)
                    ins.then_inc(rope_parts, 1)

            u = FIRST_UNIT["in0"]
            for step in EVEN_STEPS:
                if step[0] in ("unit", "cmp1"):
                    split_ahead(u)
                    u += 1
                if step == ("unit", 0, 0):
                    dve.wait_ge(wg_done, 1)
                    dve.tensor_tensor(wg_lo[:], c_wg[:], wg_hi[:].bitcast(F32), ALU.subtract).then_inc(wg_done, 1)
                elif step[0] == "unit" and step[2] == 1 and 1 <= step[1] <= 5:
                    if step[1] == 1:
                        dve.wait_ge(tables_in, 16 * TABLES)
                        dve.wait_ge(mask_cast, 1)
                    rotate(step[1])
                elif step == ("gateT",):
                    dve.wait_ge(gate_turned, 1)
                    dve.tensor_scalar(gates[:], ps[:, 6, 0:TT * NSA_HEADS * BRANCH].rearrange("p (t c) -> p t c", t=TT),
                                      0.5, 0.5, ALU.mult, ALU.add).then_inc(gate_done, 1)
                elif step == ("x2T",):
                    dve.wait_ge(x2_out, 2)
                    for kind in range(2):
                        for g in range(NSA_G):
                            v = x2[:, 2 * kind + g, :].rearrange("p (n k) -> p k n", k=8)
                            dst = xbf[:, kind, :].rearrange("p (k g n) -> p k g n", g=2, n=NC)
                            for kh in range(2):
                                ins = dve.tensor_tensor(
                                    dst[:, 8 * kh:8 * kh + 8, g, :], v[:, :, kh:kh + NC],
                                    c_pe2[:, kind, 8 * kh:8 * kh + 8].unsqueeze(2).to_broadcast([P, 8, NC]), ALU.add)
                            ins.then_inc(xb_sum, 1)
                    dve.wait_ge(xb_hid, 1)
                    dve.tensor_tensor(xb_lo[:, :, 0:CKT * 2 * NC], xbf[:],
                                      xb_hi[:, :, 0:CKT * 2 * NC].bitcast(F32), ALU.subtract).then_inc(xb_split, 1)
                elif step == ("hidT",):
                    dve.wait_ge(hid_turned, 1)
                    dve.tensor_copy(hidT[:], ps[:, 6, 0:2 * 2 * NC].rearrange("p (k n) -> p k n", k=2))
                    dve.wait_ge(vc_zero, 1)
                    for k in range(2):
                        src = ps[:, 6, (2 + k) * 2 * NC:(3 + k) * 2 * NC].rearrange("p (g n) -> p g n", g=2)
                        ins = dve.tensor_copy(
                            hidR[:, k, :, 0:NC].rearrange("p (i g) n -> p i g n", g=2),
                            src.unsqueeze(1).to_broadcast([P, NSA_PER, 2, NC]))
                    ins.then_inc(hid_out, 1)
                elif step == ("cmp2",):
                    dve.wait_ge(late_in, 16 * LATE)
                    dve.wait_ge(cmp_ready, 1)
                    half = HD // 2
                    src = ps[0:2 * NC, 7, 0:HD]
                    dve.tensor_tensor(kcr[:, 2, :], src, c_ropec[:, 0, :], ALU.mult)
                    dve.tensor_tensor(kcr[:, 3, 0:half], src[:, half:HD], c_ropec[:, 1, 0:half], ALU.mult)
                    dve.tensor_tensor(kcr[:, 3, half:HD], src[:, 0:half], c_ropec[:, 1, half:HD],
                                      ALU.mult).then_inc(kc_prod, 1)
                    dve.wait_ge(kc_prod, 1)
                    for k in range(2):
                        ins = dve.tensor_tensor(kcr[:, k, :], kcr[:, 2, :], kcr[:, 3, :], ALU.add)
                    ins.then_inc(kc_rot, 1)
                    dve.tensor_tensor(vc[:], ps[:, 6, 0:HD].unsqueeze(1).to_broadcast([P, CM, HD]),
                                      blockd[:].unsqueeze(2).to_broadcast([P, CM, HD]), ALU.mult).then_inc(vc_out, 1)
                elif step == ("kcT",):
                    dve.wait_ge(kc_turned, 1)
                    dve.wait_ge(kc_zero, 1)
                    for g in range(NSA_G):
                        rows = slice(g * HD, (g + 1) * HD)
                        ins = dve.tensor_copy(kcT[rows, g, 0:NC], ps[rows, 7, g * NC:(g + 1) * NC])
                    ins.then_inc(kc_out, 1)
                elif step == ("cscore",):
                    dve.wait_ge(cs_ready, 1)
                    for t in range(TT):
                        ins = dve.tensor_tensor(
                            pcm[:, CM * t:CM * (t + 1), 0:NC],
                            ps[:, 6, P * t:P * (t + 1)].rearrange("p (k n) -> p k n", n=NCP)[:, :, 0:NC],
                            c_cmask[:, 0, t, :].unsqueeze(1).to_broadcast([P, CM, NC]), ALU.add)
                    ins.then_inc(cs_step, 1)
                    dve.wait_ge(cs_step, 1)
                    dve.tensor_reduce(stc[:, 0, :], pcm[:, :, 0:NC], AX.X, ALU.max).then_inc(cs_step, 1)
                    dve.wait_ge(cs_step, 2)
                    dve.tensor_tensor(pcm[:, :, 0:NC], pcm[:, :, 0:NC],
                                      stc[:, 0, :].unsqueeze(2).to_broadcast([P, TT * CM, NC]),
                                      ALU.subtract).then_inc(cs_step, 2)

            def compressed_probs():
                dve.wait_ge(cs_exp, 1)
                dve.tensor_reduce(stc[:, 1, :], pcm[:, :, 0:NC], AX.X, ALU.add).then_inc(cs_step, 1)
                dve.wait_ge(cs_step, 5)
                dve.reciprocal(stc[:, 1, :], stc[:, 1, :]).then_inc(cs_step, 1)
                dve.wait_ge(cs_step, 6)
                for t in range(TT):
                    gv = gates[:, t, :].rearrange("p (g i b) -> p i g b", g=2, b=BRANCH)[:, :, :, 0]
                    o = slice(CM * t, CM * (t + 1))
                    ins = dve.tensor_tensor(stc[:, 2, o].rearrange("p (i g) -> p i g", g=2),
                                            stc[:, 1, o].rearrange("p (i g) -> p i g", g=2), gv, ALU.mult)
                ins.then_inc(cs_step, 1)
                dve.wait_ge(cs_step, 7)
                dve.tensor_tensor(pcm[:, :, 0:NC], pcm[:, :, 0:NC],
                                  stc[:, 2, :].unsqueeze(2).to_broadcast([P, TT * CM, NC]), ALU.mult).then_inc(cs_step, 1)
                dve.wait_ge(cs_step, 8)
                for t in range(TT):
                    o = slice(CM * t, CM * (t + 1))
                    ins = dve.tensor_tensor(pcm[:, o, 0:NC], pcm[:, o, 0:NC],
                                            c_cmask[:, 1, t, :].unsqueeze(1).to_broadcast([P, CM, NC]), ALU.mult)
                ins.then_inc(cs_step, 1)

            def it_maxima(n):
                kind, _, t = ITEMS[n]
                s, w, o, m = n % 4, P * (t + 1), s_half(n), maps_of(n)
                dve.wait_ge(it_scores, n + 1)
                if kind == "dil":
                    dve.tensor_reduce(stat[:, s, 0:1], psh[:, o:o + m, 0:w], AX.XY, ALU.max,
                                      negate=True).then_inc(it_max, 1)
                else:
                    dve.tensor_reduce(stat[:, s, 0:4], psh[:, o:o + 4, 0:w], AX.X, ALU.max,
                                      negate=True).then_inc(it_max, 1)

            def it_turned_out(n):
                if ITEMS[n][2] == 0:
                    return
                k = maps_of(n) * 2 * P
                dve.wait_ge(it_turned, n + 1)
                if n >= 2:
                    dve.wait_ge(it_pv, n - 1)
                dve.tensor_copy(probsT[:, n % 2, BLK:k], ps[:, 5, 0:k - BLK]).then_inc(it_pT1, 1)

            exps = [sum(1 if ITEMS[k][0] == "dil" else 4 for k in range(n + 1)) for n in range(NI)]
            done = {"coef": 0, "o": 0}

            def it_output(n):
                kind, j, t = ITEMS[n]
                v, s = n % 4, n % 2
                dve.wait_ge(it_exp, exps[n])
                if kind == "dil":
                    dve.reciprocal(coef[:, s, 0:1], stat[:, v, 4:5]).then_inc(it_coef, 1)
                    done["coef"] += 1
                    dve.wait_ge(it_coef, done["coef"])
                    dve.wait_ge(it_pv, n + 1)
                    col = (TILE_OF[n] * 2 + j % 2) * HD
                    dve.tensor_scalar(xn[:, t, col:col + HD], ps[:, 6 + s, 0:HD], coef[:, s, 0:1], None,
                                      ALU.mult).then_inc(it_o, 1)
                    done["o"] += 1
                    return
                dve.reciprocal(coef[:, s, 0:4], stat[:, v, 4:8]).then_inc(it_coef, 1)
                dve.wait_ge(it_coef, done["coef"] + 1)
                gv = gates[:, t, :].rearrange("p (g i b) -> p g i b", g=2, b=BRANCH)[:, :, j, 1:3]
                dve.tensor_tensor(coef[:, s, 4:8].rearrange("p (g b) -> p g b", g=2),
                                  coef[:, s, 0:4].rearrange("p (g b) -> p g b", g=2), gv, ALU.mult).then_inc(it_coef, 1)
                done["coef"] += 2
                dve.wait_ge(it_coef, done["coef"])
                dve.wait_ge(it_pv, n + 1)
                dve.wait_ge(oc_out, t + 1)
                for br in range(2):
                    for g in range(NSA_G):
                        m, col = 2 * g + br, (2 * (NSA0 + j) + g) * HD
                        ins = dve.scalar_tensor_tensor(xn[:, t, col:col + HD], ps[:, 6 + s, m * HD:(m + 1) * HD],
                                                       coef[:, s, 4 + m:5 + m], xn[:, t, col:col + HD], ALU.mult,
                                                       ALU.add)
                    ins.then_inc(it_o, 1)
                    done["o"] += 1
                    if br == 0:
                        dve.wait_ge(it_o, done["o"])

            def it_lo(n):
                tile = TILE_OF[n]
                dve.wait_ge(ot_hi, turns_before(n) + 1)
                dve.tensor_tensor(xlo[:, tile, :], ps[:, 6 + n % 2, SEQ:2 * SEQ], xhi[:, tile, :].bitcast(F32),
                                  ALU.subtract).then_inc(ot_lo, 1)

            it_maxima(0)
            it_maxima(1)
            compressed_probs()
            for n in range(NI + 2):
                if n < NI:
                    it_turned_out(n)
                if n + 2 < NI:
                    it_maxima(n + 2)
                if n == PC_TURN:
                    dve.wait_ge(pc_turned, 1)
                    dve.tensor_copy(pcT[:], ps[:, 5, 0:TT * P].rearrange("p (t c) -> p t c", t=TT)).then_inc(pc_out, 1)
                elif n in PC_VALUES:
                    t = PC_VALUES.index(n)
                    dve.wait_ge(oc_ready, t + 1)
                    dve.tensor_copy(xn[:, t, NSA0 * P:NSA0 * P + BLK], ps[:, 5, :]).then_inc(oc_out, 1)
                if n - 2 in TURNS:
                    it_lo(n - 2)
                if 1 <= n <= NI:
                    it_output(n - 1)
                if n in SPLIT_AT:
                    k = SPLIT_AT.index(n)
                    split_half(FIRST_UNIT["out0"] + LOOK + k // 2, k % 2)

            def plain_stage(name, ahead=0):
                for u in range(FIRST_UNIT[name] + ahead, FIRST_UNIT[name] + dict(STAGES)[name]):
                    split_ahead(u)

            plain_stage("out0", 2)
            junction(0)

            def ffn(layer):
                u0, k0 = FIRST_UNIT[f"up{layer}"], layer * UP_CHUNKS

                def taps(par, at, cofs):
                    for bank in range(2):
                        dve.wait_ge(up_ident, 4 * (k0 + at) + 2 * (bank + 1))
                        for m in (2 * bank, 2 * bank + 1):
                            ins = dve.scalar_tensor_tensor(
                                conv[:, par, m, 1:SEQ], psh[:, 4 * par + m, 0:SEQ - 1],
                                c_conv[:, bass.ds(cofs + (4 * m + 1), 1)], conv[:, par, m, 1:SEQ], ALU.mult, ALU.add)
                        ins.then_inc(up_tap1, 1)
                    for bank in range(2):
                        dve.wait_ge(up_tap1, 2 * (k0 + at) + (bank + 1))
                        for m in (2 * bank, 2 * bank + 1):
                            ins = dve.scalar_tensor_tensor(
                                conv[:, par, m, 2:SEQ], psh[:, 4 * par + m, 0:SEQ - 2],
                                c_conv[:, bass.ds(cofs + 4 * m, 1)], conv[:, par, m, 2:SEQ], ALU.mult, ALU.add)
                    ins.then_inc(up_free, 1)

                split_ahead(u0)
                split_ahead(u0 + 1)
                taps(0, 0, layer * UP_CHUNKS * 16)
                with dve.Fori(0, (UP_CHUNKS - 1) // 2) as i:
                    for j in range(2):
                        for half in range(2):
                            v = u0 + 2 + 2 * j + half + LOOK
                            split(v % RING, 4 * i + v)
                        taps((1 + j) % 2, 2 * i + (1 + j), (2 * i + (1 + j)) * 16 + layer * UP_CHUNKS * 16)
                plain_stage(f"down{layer}")
                junction(2 * layer + 1)

            ffn(0)

            def sb_minus_abs(n):
                z = ps[:, sb_bank(n):sb_bank(n) + 2, 0:384].bitcast(U32)
                dve.wait_ge(sb_z, n + 1)
                if n >= 3:
                    dve.wait_ge(sb_spl, n - 2)
                dve.tensor_scalar(sb_sp[:, n % 3].bitcast(U32), z, 0x80000000, None, ALU.bitwise_or).then_inc(sb_absd, 1)

            def sb_softplus(n):
                sp = sb_sp[:, n % 3]
                dve.wait_ge(sb_ln, n + 1)
                dve.scalar_tensor_tensor(sp, ps[:, sb_bank(n):sb_bank(n) + 2, 0:384], 0.0, sp, ALU.max,
                                         ALU.add).then_inc(sb_spd, 1)

            def sb_softplus_lo(n):
                dve.wait_ge(sb_sph, n + 1)
                dve.tensor_tensor(sb_splo[:, n % 2], sb_sp[:, n % 3], sb_sphi[:, n % 2].bitcast(F32),
                                  ALU.subtract).then_inc(sb_spl, 1)

            def sb_lo(n):
                dve.wait_ge(sb_ohi, n + 1)
                dve.tensor_tensor(xlo[:, n, :], ps[:, 6 + n % 2, 0:SEQ], xhi[:, n, :].bitcast(F32),
                                  ALU.subtract).then_inc(sb_olo, 1)

            u = FIRST_UNIT["in1"]
            for step in ODD_STEPS:
                if step[0] == "unit":
                    split_ahead(u)
                    u += 1
                    if step == ("unit", 5, 0):
                        sb_minus_abs(0)
                        sb_softplus(0)
                        sb_minus_abs(1)
                    elif step == ("unit", 5, 1):
                        sb_softplus_lo(0)
                    if step[1] in ODD_TILE and step[2] == 1:
                        c = step[1]
                        dve.wait_ge(unit_used, ODD_END["unit", c])
                        b0 = 4 * (c % 2)
                        dve.tensor_scalar(qkT[:, ODD_TILE[c]:ODD_TILE[c] + 4, :], psh[:, b0:b0 + 4, :],
                                          SCALE if c % 2 else 1.0, None, ALU.mult).then_inc(turned_out, 1)

            sb_minus_abs(2)
            for n in range(NP + 2):
                if n + 1 < NP:
                    sb_softplus(n + 1)
                if n >= 2:
                    sb_lo(n - 2)
                if n + 1 < NP:
                    sb_softplus_lo(n + 1)
                if n + 3 < NP:
                    sb_minus_abs(n + 3)
            plain_stage("out1")
            junction(2)
            ffn(1)

        @block.gpsimd
        def _(pool):
            pool.memset(mhalf[:], -0.5).then_inc(half_set, 1)
            pool.wait_ge(half_set, 1)
            pool.sem_inc(up_free, 1)
            pool.sem_inc(up_hf, 1)

            def power(p, which, t, ready, done):
                pool.wait_ge(ready, TT * p + t + 1)
                pool.tensor_tensor(rstd[:, which, t:t + 1], ms[:, which, t:t + 1], mhalf[:], ALU.pow).then_inc(done, 1)

            for t in range(TT):
                power(0, 0, t, pre_ms, pre_rstd)
            pool.wait_ge(ident_in, 16)
            pool.wait_ge(tables_in, 16 * TABLES)
            pool.tensor_copy(c_mask[:], mask_f)
            pool.tensor_copy(c_identb[:], c_identf[:]).then_inc(mask_cast, 1)
            pool.memset(xb_hi[:, :, CKT * 2 * NC:].bitcast(F32), 0.0)
            pool.memset(xb_lo[:, :, CKT * 2 * NC:].bitcast(F32), 0.0).then_inc(xb_pad, 1)
            pool.memset(kcT[:], 0.0).then_inc(kc_zero, 1)
            pool.memset(hidR[:, :, :, NC:], 0.0).then_inc(vc_zero, 1)
            pool.memset(pcm[:, :, NC:], 0.0).then_inc(vc_zero, 1)
            for c in range(1, 6):
                n = 256 if c == 5 else 512
                for t in range(TT):
                    pool.wait_ge(rope_parts, TT * (c - 1) + t + 1)
                    if c == 2 and t == 0:
                        pool.wait_ge(x2_turned, 1)
                    if c >= 3 and t == 0:
                        pool.wait_ge(turned, c - 2)
                    pool.tensor_tensor(xn[:, c % 2, t * BLK:t * BLK + n], t12[:, 0, t, 0:n], t12[:, 1, t, 0:n],
                                       ALU.add).then_inc(staged, 1)
            def junction(p):
                for t in range(TT):
                    power(p, 1, t, post_ms, post_rstd)
                    if p < 3:
                        power(p + 1, 0, t, pre_ms, pre_rstd)

            junction(0)

            def ffn(layer):
                k0 = layer * UP_CHUNKS

                def hidden(par, at, tile):
                    pool.wait_ge(up_gelu, k0 + 1 + at)
                    pool.tensor_tensor(hidf[:, par], act_g[:, par], conv[:, par, 2:4, :], ALU.mult).then_inc(up_hf, 1)
                    pool.wait_ge(up_hi, k0 + 1 + at)
                    pool.tensor_tensor(hid_lo[:, tile, :], hidf[:, par], hid_hi[:, tile, :].bitcast(F32),
                                       ALU.subtract).then_inc(up_lo, 1)

                with pool.Fori(0, (UP_CHUNKS - 1) // 2) as i:
                    for j in range(2):
                        hidden(j, 2 * i + j, bass.ds(4 * i + 2 * j, 2))
                last = UP_CHUNKS - 1
                hidden(last % 2, last, slice(2 * last, 2 * last + 2))
                junction(2 * layer + 1)

            ffn(0)
            pool.wait_ge(pre_tr, 2 * TT * 3)
            pool.tensor_copy(tri_r, c_tri[:]).then_inc(tri_cast, 1)
            junction(2)
            ffn(1)

        @block.tensor
        def _(pe):
            def pre(p, t):
                for c in range(2):
                    pe.wait_ge(pre_xn, 2 * (p * TT + t) + c + 1)
                    for k in range(4 * c, 4 * c + 4):
                        ins = pe.transpose(psq[:, 4 * T_BANK[p] + 8 * t + k, :], xn[:, t, k * P:(k + 1) * P], c_identf[:])
                    ins.then_inc(pre_tr, 1)

            def three(out, s_hi, s_lo, m_hi, m_lo, start, stop, shared=False):
                pe.matmul(out, s_hi, m_hi, start=start, stop=False, skip_group_check=shared)
                pe.matmul(out, s_hi, m_lo, start=False, stop=False, skip_group_check=shared)
                return pe.matmul(out, s_lo, m_hi, start=False, stop=stop, skip_group_check=shared)

            def tile_block(slot, b, kt, ohi, olo, t, out, start, stop):
                cols, tok = slice(b * BLK, (b + 1) * BLK), slice(t * P, (t + 1) * P)
                return three(out, ohi[:, kt, tok], olo[:, kt, tok], whi[:, slot, cols], wlo[:, slot, cols], start, stop)

            def token_block(slot, b, kt, ohi, olo, banks, start, stop):
                for t in range(TT):
                    ins = tile_block(slot, b, kt, ohi, olo, t, ps[:, banks[t], :], start, stop)
                return ins

            def in_unit(u, bank, half):
                slot = u % RING
                pe.wait_ge(lo_done, u + 1)
                for b in range(4):
                    kt = 4 * half + b
                    ins = token_block(slot, b, kt, xhi, xlo, (bank, bank + 1), kt == 0, kt == KT - 1)
                ins.then_inc(unit_used, 1)

            def channel_blocks(slot, par, half):
                for m in range(4):
                    for b in range(4):
                        kt = 4 * half + b
                        cols = slice(b * BLK + m * P, b * BLK + (m + 1) * P)
                        ins = three(psh[:, 4 * par + m, :], whi[:, slot, cols], wlo[:, slot, cols],
                                    xhi[:, kt, :], xlo[:, kt, :], kt == 0 and m % 2 == 0, kt == KT - 1, True)
                ins.then_inc(unit_used, 1)

            def channel_unit(u, par, half):
                pe.wait_ge(lo_done, u + 1)
                channel_blocks(u % RING, par, half)

            def first_units(u0, p, bank=0, tile_ready=None):
                for t in range(TT):
                    for kt in range(KT):
                        u, b = u0 + kt // 4, kt % 4
                        if t == 0 and kt == KT - 2:
                            pre(p, 1)
                        if b == 0:
                            pe.wait_ge(pre_lo, 2 * (p * TT + t) + kt // 4 + 1)
                            if p > 0:
                                pe.wait_ge(lo_done, u + 1)
                            elif t == 0:
                                pe.wait_ge(first_lo, u + 1)
                        elif b == 2 and p == 0 and t == 0:
                            pe.wait_ge(lo_done, u + 1)
                        ins = tile_block(u % RING, b, kt, xhi, xlo, t, ps[:, bank + t, :], kt == 0, kt == KT - 1)
                        if t == TT - 1 and b == 3:
                            ins.then_inc(unit_used, 1)
                    if t == 0 and tile_ready is not None:
                        ins.then_inc(tile_ready, 1)

            def out_blocks(name, p, kts, ohi, olo, first, last, ready=None, tiles=range(TT)):
                u0, y0 = FIRST_UNIT[name], Y_BANK[p]
                for blk in range(first, last):
                    c, kt, u, b = blk // kts, blk % kts, u0 + blk // 4, blk % 4
                    if b == 0 or blk == first:
                        pe.wait_ge(lo_done, u + 1)
                    if ready is not None and c == 0:
                        ready(kt, tiles)
                    for t in tiles:
                        ins = tile_block(u % RING, b, kt, ohi, olo, t, ps[:, y0 + 2 * t + c, :], kt == 0, kt == kts - 1)
                        if kt == kts - 1:
                            ins.then_inc(y_done[t], 1)
                    if b == 3 and tiles[-1] == TT - 1:
                        if kt == kts - 1:
                            pe.wait_ge(y_done[TT - 1], 2 * p + c + 1)
                            pe.sem_inc(unit_used, 1)
                        else:
                            ins.then_inc(unit_used, 1)

            def out_proj(name, p, kts, ohi, olo, first, ready=None):
                tail = 2 * kts - 8
                out_blocks(name, p, kts, ohi, olo, first, tail, ready)
                for t in range(TT):
                    out_blocks(name, p, kts, ohi, olo, max(first, tail), 2 * kts, ready, (t,))

            pe.wait_ge(ident_in, 16)
            pre(0, 0)

            def it_qk(n):
                kind, j, t = ITEMS[n]
                o, w = s_half(n), P * (t + 1)
                tok = slice(t * P, (t + 1) * P)
                if n >= 2:
                    pe.wait_ge(it_exp, exps[n - 2])
                if kind == "dil":
                    for g in range(NG):
                        hd = g * SLOTS + j
                        rows = slice(HD * (hd % 2), HD * (hd % 2) + HD)
                        pe.matmul(psh[:, o + g, 0:w], qkT[rows, TDQ + hd // 2, tok], qkT[rows, TDK + hd // 2, 0:w],
                                  start=g != 1, stop=False, skip_group_check=True)
                    msk = c_mask[:, 0:NG, :] if t else c_mask[:, 0:NG, P:SEQ]
                    pe.matmul(psh[:, o:o + 2, 0:w], c_identb[:], msk[:, 0:2, :], start=False, stop=True,
                              skip_group_check=True)
                    pe.matmul(psh[:, o + 2, 0:w], c_identb[:], msk[:, 2, :], start=False, stop=True,
                              skip_group_check=True).then_inc(it_scores, 1)
                    return
                for g in range(NSA_G):
                    rows = slice(g * HD, (g + 1) * HD)
                    pe.matmul(psh[:, o + 2 * g:o + 2 * g + 2, 0:w], qkT[rows, TQ + j, tok],
                              qkT[rows, TSLC:TWIN + 1, 0:w], start=True, stop=False, skip_group_check=True)
                for g in range(NSA_G):
                    ins = pe.matmul(psh[:, o + 2 * g:o + 2 * g + 2, w - P:w], c_identb[:],
                                    c_mask[:, 0:1, P:SEQ].to_broadcast([P, 2, P]), start=False, stop=True,
                                    skip_group_check=True)
                ins.then_inc(it_scores, 1)

            def it_turn(n):
                t = ITEMS[n][2]
                w = P * (t + 1)
                pe.wait_ge(it_exp, exps[n])
                if n >= 1:
                    pe.wait_ge(it_pT0, n)
                if t and wide_before(n):
                    pe.wait_ge(it_pT1, wide_before(n))
                if n == PC_TURN + 1:
                    pe.wait_ge(pc_out, 1)
                elif n - 1 in PC_VALUES:
                    pe.wait_ge(oc_out, PC_VALUES.index(n - 1) + 1)
                blk = 0
                for m in range(maps_of(n)):
                    for k in range(t + 1):
                        ins = pe.transpose(psq[:, 16 + blk, :], probs[:, n % 2, m * w + k * P:m * w + (k + 1) * P],
                                           c_identf[:])
                        blk += 1
                ins.then_inc(it_turned, 1)

            def compressed_turn():
                pe.wait_ge(it_pT1, wide_before(PC_TURN))
                pe.wait_ge(cs_step, 9)
                pe.wait_ge(vc_zero, 2)
                for t in range(TT):
                    ins = pe.transpose(psq[:, 20 + t, :], pcm[:, CM * t:CM * (t + 1), :].rearrange("p m n -> p (m n)"),
                                       c_identf[:])
                ins.then_inc(pc_turned, 1)

            def compressed_values(n):
                pe.wait_ge(it_pT1, wide_before(n))
                pe.wait_ge(pc_out, 1)
                pe.matmul(ps[:, 5, :], pcT[:, PC_VALUES.index(n), :], vc[:].rearrange("p m d -> p (m d)"), start=True,
                          stop=True).then_inc(oc_ready, 1)

            def it_values(n):
                kind, j, t = ITEMS[n]
                s, bank = n % 2, 6 + n % 2
                pe.wait_ge(it_pT0, n + 1)
                if t:
                    pe.wait_ge(it_pT1, wide_before(n) + 1)
                if n >= 2:
                    pe.wait_ge(it_o, outs[n - 2])
                    if n - 2 in TURNS:
                        pe.wait_ge(ot_lo, turns_before(n - 2) + 1)
                maps = maps_of(n)
                for m in range(maps):
                    if kind == "dil":
                        v0, col = V_DIL + (m * SLOTS + j) * HD, 0
                    else:
                        v0, col = (V_SLC, V_WIN)[m % 2] + (m // 2) * HD, m * HD
                    for kt in range(t + 1):
                        k = m * (t + 1) + kt
                        ins = pe.matmul(ps[:, bank, col:col + HD], probsT[:, s, k * P:(k + 1) * P],
                                        vbuf[:, kt, v0:v0 + HD], start=k == 0, stop=k == maps * (t + 1) - 1,
                                        skip_group_check=True)
                ins.then_inc(it_pv, 1)

            def out_turn(n):
                tile = TILE_OF[n]
                pe.wait_ge(it_o, outs[n])
                for t in range(TT):
                    ins = pe.transpose(psq[:, 4 * (6 + n % 2) + 2 + t, :], xn[:, t, tile * P:(tile + 1) * P], c_identf[:])
                ins.then_inc(ot_turned, 1)

            exps = [sum(1 if ITEMS[k][0] == "dil" else 4 for k in range(n + 1)) for n in range(NI)]
            outs = [sum(1 if ITEMS[k][0] == "dil" else 2 for k in range(n + 1)) for n in range(NI)]
            u = FIRST_UNIT["in0"]
            for step in EVEN_STEPS:
                if step == ("unit", 6, 1):
                    pe.wait_ge(mask_cast, 1)
                    pe.wait_ge(turned_out, 5)
                    pe.wait_ge(in_free_act, EVEN_ACT - 1)
                    it_qk(0)
                    it_qk(1)
                if step[0] == "unit":
                    c, half = step[1:]
                    if c >= 2 and half == 0:
                        if c == 2:
                            pe.wait_ge(in_free_act, 1)
                        else:
                            pe.wait_ge(rope_parts, TT * (c - 2))
                    if c == 6:
                        if half == 0:
                            pe.wait_ge(cs_step, 1)
                        in_unit(u, 6, half)
                    elif c > 0:
                        in_unit(u, 2 * (c % 2), half)
                    elif half == 1:
                        first_units(u - 1, 0)
                    u += 1
                elif step == ("gate",):
                    pe.wait_ge(wg_done, 2)
                    for kt in range(KT):
                        ins = three(ps[0:NSA_HEADS * BRANCH, 7, 0:SEQ], wg_hi[:, kt, :], wg_lo[:, kt, :], xhi[:, kt, :],
                                    xlo[:, kt, :], kt == 0, kt == KT - 1)
                    ins.then_inc(gate_ready, 1)
                elif step == ("gateT",):
                    pe.wait_ge(gate_tanh, 1)
                    for t in range(TT):
                        n = NSA_HEADS * BRANCH
                        ins = pe.transpose(ps[:, 6, t * n:(t + 1) * n], gatesT[:, t * P:(t + 1) * P], c_identf[0:n, 0:n])
                    ins.then_inc(gate_turned, 1)
                elif step == ("x2T",):
                    pe.wait_ge(in_free_act, 1)
                    pe.wait_ge(gate_done, 1)
                    for kg in range(4):
                        for t in range(TT):
                            src = xn[:, 0, t * BLK + kg * P:t * BLK + (kg + 1) * P]
                            ins = pe.transpose(psq[:, 24 + 2 * kg + t, :], src, c_identf[:])
                    ins.then_inc(x2_turned, 1)
                elif step[0] == "turn":
                    c = step[1]
                    pe.wait_ge(staged, TT * c)
                    if c >= 2:
                        pe.wait_ge(turned_out, c - 1)
                    for tile in range(2 if c == 5 else 4):
                        for t in range(TT):
                            ins = pe.transpose(psq[:, 16 + 2 * tile + t, :],
                                               xn[:, c % 2, t * BLK + tile * P:t * BLK + (tile + 1) * P], c_identf[:])
                    ins.then_inc(turned, 1)
                elif step[0] == "cmp1":
                    kind, half = step[1:]
                    if half == 0:
                        pe.wait_ge(xb_split, 1)
                        pe.wait_ge(xb_pad, 1)
                    pe.wait_ge(lo_done, u + 1)
                    for b in range(8):
                        kt = 8 * half + b
                        win = slice(kt * 2 * NC, kt * 2 * NC + P)
                        cols = slice(b * CMP_H, (b + 1) * CMP_H)
                        ins = three(ps[:, 6 + kind, 0:CMP_H], xb_hi[:, kind, win], xb_lo[:, kind, win],
                                    whi[:, u % RING, cols], wlo[:, u % RING, cols], kt == 0, kt == CKT - 1)
                    ins.then_inc(unit_used, 1)
                    u += 1
                elif step == ("hidT",):
                    pe.wait_ge(hid_gelu, 1)
                    for kind in range(2):
                        for k in range(2):
                            o = (2 * kind + k) * 2 * NC
                            ins = pe.transpose(ps[:, 6, o:o + 2 * NC], hid[:, kind, k * P:(k + 1) * P],
                                               c_identf[0:2 * NC, 0:2 * NC])
                    ins.then_inc(hid_turned, 1)
                elif step == ("cmp2",):
                    pe.wait_ge(late_in, 16 * LATE)
                    pe.wait_ge(hid_out, 1)
                    for k in range(2):
                        pe.matmul(ps[0:2 * NC, 7, 0:HD], hidT[:, k, :], c_w2[:, 0, k, :], start=k == 0, stop=k == 1)
                    for k in range(2):
                        ins = pe.matmul(ps[:, 6, 0:HD], hidR[:, k, :, :].rearrange("p m n -> p (m n)"), c_w2[:, 1, k, :],
                                        start=k == 0, stop=k == 1)
                    ins.then_inc(cmp_ready, 1)
                elif step == ("kcT",):
                    pe.wait_ge(kc_rot, 1)
                    pe.transpose(ps[:, 7, 0:2 * NC], kcr[:, 0:2, :].rearrange("p k d -> p (k d)"), c_identf[0:2 * NC, 0:2 * NC]).then_inc(kc_turned, 1)
                elif step == ("cscore",):
                    pe.wait_ge(kc_out, 1)
                    pe.wait_ge(vc_out, 1)
                    pe.wait_ge(turned_out, 1)
                    for t in range(TT):
                        for i in range(NSA_PER):
                            o = (NSA_PER * t + i) * 2 * NCP
                            ins = pe.matmul(ps[:, 6, o:o + 2 * NCP], qkT[:, TQ + i, t * P:(t + 1) * P],
                                            kcT[:].rearrange("p g n -> p (g n)"), start=True, stop=True)
                    ins.then_inc(cs_ready, 1)

            for n in range(NI):
                it_turn(n)
                if n == 1:
                    pe.wait_ge(in_free_act, EVEN_ACT)
                if n + 2 < NI:
                    it_qk(n + 2)
                if n == PC_TURN:
                    compressed_turn()
                elif n in PC_VALUES:
                    compressed_values(n)
                if n - 2 in TURNS:
                    out_turn(n - 2)
                if n >= 1:
                    it_values(n - 1)

            def operand(kt, tiles):
                n = max(m for m in TURNS if TILE_OF[m] == kt)
                pe.wait_ge(ot_lo, turns_before(n) + 1)

            out_blocks("out0", 0, EVEN_KT, xhi, xlo, 0, 2, operand)
            it_values(NI - 1)
            out_blocks("out0", 0, EVEN_KT, xhi, xlo, 2, 3, operand)
            out_turn(NI - 1)
            out_blocks("out0", 0, EVEN_KT, xhi, xlo, 3, 4, operand)
            out_proj("out0", 0, EVEN_KT, xhi, xlo, 4, operand)

            def ffn(layer):
                pre(2 * layer + 1, 0)
                u0, k0 = FIRST_UNIT[f"up{layer}"], layer * UP_CHUNKS

                def up_chunk(par, slots, at):
                    for half in range(2):
                        pe.wait_ge(lo_done, at[half] + 1)
                        channel_blocks(slots[half], par, half)

                first_units(u0, 2 * layer + 1, UP_BANK[layer], up_tok)
                for t in range(TT):
                    pe.wait_ge(up_staged, TT * layer + t + 1)
                    for m in range(4):
                        ins = pe.transpose(psh[:, m, t * P:(t + 1) * P], xn[:, t, m * P:(m + 1) * P], c_identf[:])
                ins.then_inc(up_turned, 1)
                with pe.Fori(0, (UP_CHUNKS - 1) // 2) as i:
                    for j in range(2):
                        v = u0 + 2 + 2 * j
                        if j == 1:
                            pe.wait_ge(up_free, 1 + k0 + 2 * i + 1)
                        else:
                            pe.wait_ge(up_free, 1 + k0 + 2 * i)
                        up_chunk((1 + j) % 2, (v % RING, (v + 1) % RING), (4 * i + v, 4 * i + v + 1))
                out_proj(f"down{layer}", 2 * layer + 1, FT, hid_hi, hid_lo, 0,
                         lambda kt, tiles: pe.wait_ge(up_lo, k0 + kt // 2 + 1))

            ffn(0)

            def sb_scores(n):
                s = sb_bank(n)
                if n >= 3:
                    pe.wait_ge(sb_prob, n - 2)
                for hd in range(2):
                    rows, bank = slice(HD * hd, HD * hd + HD), s + hd
                    pe.matmul(ps[:, bank, 0:SEQ], qkT[rows, NP + n, 0:P], qkT[rows, n, :], start=True, stop=False,
                              skip_group_check=True)
                    pe.matmul(ps[:, bank, SEQ:SEQ + P], qkT[rows, NP + n, P:SEQ], qkT[rows, n, P:SEQ], start=False,
                              stop=False, skip_group_check=True)
                for hd in range(2):
                    diag = psq[:, 4 * (s + hd):4 * (s + hd) + 3:2, :]
                    ins = pe.matmul(diag, c_identb[:], c_mask[:, NG:NG + 1, 0:P].to_broadcast([P, 2, P]), start=False,
                                    stop=False, skip_group_check=True)
                ins.then_inc(sb_z, 1)

            def sb_sums(n):
                s = sb_bank(n)
                pe.wait_ge(sb_spl, n + 1)
                for hd in range(2):
                    for part in (sb_sphi, sb_splo):
                        pe.matmul(ps[:, s + hd, 0:384], tri_r[:, 0, :], part[:, n % 2, hd, :], start=False, stop=False,
                                  skip_group_check=True)
                        ins = pe.matmul(ps[:, s + hd, P:SEQ], tri_r[:, 1, :], part[:, n % 2, hd, SEQ:SEQ + P],
                                        start=False, stop=part is sb_splo, skip_group_check=True)
                ins.then_inc(sb_cum, 1)

            def sb_values(n):
                pe.wait_ge(sb_prob, n + 1)
                if n >= 2:
                    pe.wait_ge(sb_olo, n - 1)
                for hd in range(2):
                    v0 = (2 * n + hd) * HD
                    o = ps[HD * hd:HD * hd + HD, 6 + n % 2, :]
                    pe.matmul(o[:, 0:SEQ], vbuf[:, 0, v0:v0 + HD], sb_a[:, n % 2, hd, 0:SEQ], start=True, stop=False)
                    ins = pe.matmul(o[:, P:SEQ], vbuf[:, 1, v0:v0 + HD], sb_a[:, n % 2, hd, SEQ:SEQ + P], start=False,
                                    stop=True)
                ins.then_inc(sb_pv, 1)

            pre(2, 0)
            u = FIRST_UNIT["in1"]
            for step in ODD_STEPS:
                if step[0] == "unit":
                    c, half = step[1:]
                    if c == 5:
                        pe.wait_ge(turned_out, EVEN_ROT + (2 if half == 0 else 4))
                        sb_scores(half)
                    if c >= 2 and half == 0:
                        if c == 2:
                            pe.wait_ge(in_free_act, EVEN_ACT + 1)
                        else:
                            pe.wait_ge(turned_out, EVEN_ROT + c - 2)
                    if c in ODD_TILE:
                        channel_unit(u, c % 2, half)
                    elif c == 5:
                        in_unit(u, 2, half)
                    elif half == 1:
                        first_units(u - 1, 2)
                    u += 1

            pe.wait_ge(tri_cast, 1)
            pe.wait_ge(in_free_act, EVEN_ACT + 2)
            sb_scores(2)
            for n in range(NP):
                sb_sums(n)
                if n >= 1:
                    sb_values(n - 1)
                if n + 3 < NP:
                    sb_scores(n + 3)

            def pairs(kt, tiles):
                pe.wait_ge(sb_olo, kt + 1)

            out_blocks("out1", 2, KT, xhi, xlo, 0, 2, pairs)
            sb_values(NP - 1)
            out_blocks("out1", 2, KT, xhi, xlo, 2, 4, pairs)
            out_proj("out1", 2, KT, xhi, xlo, 4, pairs)
            ffn(1)


def lay_out(x, norm_g, even_w_in, even_w_out, cmp_pe, cmp_w1, cmp_w2, odd_w_in, odd_w_out, ffn_w_up, ffn_conv_w,
            ffn_conv_b, ffn_w_down):
    f32 = np.float32

    def blocks_in(w):
        k, n = w.shape
        v = w.reshape(k // (4 * P), 4, P, n // BLK, BLK)
        return v.transpose(3, 0, 2, 1, 4).reshape(-1, P, UNIT)

    def blocks_out(w):
        k, n = w.shape
        v = w.reshape(k // P, P, n // BLK, BLK).transpose(2, 0, 1, 3).reshape(-1, 4, P, BLK)
        return v.transpose(0, 2, 1, 3).reshape(-1, P, UNIT)

    w = even_w_in[0]
    kv = NSA_HEADS * HD
    gate0 = kv + 2 * BRANCH * NSA_G * HD
    dil0 = gate0 + NSA_HEADS * BRANCH
    ndil = NG * SLOTS * HD
    pair = [e for i in range(NSA_PER) for e in (i, NSA_PER + i)]
    kvc = [w[:, kv + j * P:kv + (j + 1) * P] for j in range(2 * BRANCH)]
    q = w[:, :kv].reshape(D, NSA_HEADS, HD)[:, pair].reshape(D, kv)
    w_in0 = np.concatenate([kvc[0], kvc[1], kvc[3], kvc[5], q, w[:, dil0:dil0 + 2 * ndil], kvc[2], kvc[4],
                            w[:, dil0 + 2 * ndil:]], axis=1)
    in0 = blocks_in(w_in0)
    c1 = cmp_w1[0].reshape(2, 2, 8, P, CMP_H).transpose(0, 1, 3, 2, 4).reshape(4, P, UNIT)
    w_out0 = np.concatenate([even_w_out[0][kv:], even_w_out[0][:kv].reshape(NSA_HEADS, HD, D)[pair].reshape(kv, D)])

    q, k, v = (odd_w_in[0][:, i * D:(i + 1) * D] for i in range(3))
    w_in1 = np.concatenate([v[:, :BLK], q[:, :BLK], k[:, :BLK], q[:, BLK:], k[:, BLK:], v[:, BLK:]], axis=1)

    def up(layer):
        v = ffn_w_up[layer].reshape(D, 2, UP_CHUNKS, 2 * P).transpose(0, 2, 1, 3).reshape(D, 2 * D_FF)
        return blocks_in(v)

    weights = np.concatenate([in0[:6], c1[:2], in0[6:8], c1[2:], in0[8:], blocks_out(w_out0), up(0),
                              blocks_out(ffn_w_down[0]), blocks_in(w_in1), blocks_out(odd_w_out[0]), up(1),
                              blocks_out(ffn_w_down[1])])
    assert weights.shape == (NUNITS, P, UNIT)

    wgate = w[:, gate0:dil0].reshape(KT, P, NSA_HEADS * BRANCH).transpose(1, 0, 2)
    cmpw2 = cmp_w2[0].reshape(2, 2, P, HD).transpose(2, 0, 1, 3)
    pe2 = cmp_pe[0].reshape(2, CKT, 2, HD).transpose(2, 3, 0, 1).reshape(P, 2, CKT)
    gpre = norm_g[:, 0::2].reshape(4, D)
    gpost = norm_g[:, 1::2].reshape(4, D)
    taps = np.concatenate([ffn_conv_w, ffn_conv_b[:, None]], axis=1)
    convw = taps.reshape(2, 4, 2, UP_CHUNKS, 2, P).transpose(5, 0, 3, 2, 4, 1).reshape(P, -1)

    def rotary(pos):
        inv = np.power(f32(10000.0), -np.arange(HD // 2, dtype=f32) / f32(HD // 2)).astype(f32)
        ang = pos.astype(f32)[:, None] * inv[None, :]
        cos, sin = np.cos(ang), np.sin(ang)
        return np.stack([np.concatenate([cos, cos], 1), np.concatenate([-sin, sin], 1)])

    tab = rotary(np.arange(SEQ)).reshape(2, TT, P, HD).transpose(2, 0, 1, 3)
    rope = np.stack([tab * f32(SCALE), tab], axis=1)
    ends = np.arange(NC) * CMP_STRIDE + CMP_LEN - 1
    ropec = np.tile(rotary(ends), (1, 2, 1)).transpose(1, 0, 2)
    seen = ends[None, :] <= np.arange(SEQ)[:, None]
    cmask = np.stack([np.where(seen, 0.0, NEG), seen]).reshape(2, TT, P, NC).transpose(2, 0, 1, 3)
    t, k = P + np.arange(P)[:, None], np.arange(SEQ)[None, :]
    ok = [(k <= t) & (t - k <= win) & ((t - k) % dil == 0) for win, dil in zip(DIL_WINDOW, DIL)]
    ok.append(np.arange(P)[:, None] < np.arange(SEQ)[None, :])
    masks = np.where(np.stack(ok, 1), 0.0, NEG)
    tri = -np.stack([np.arange(P)[:, None] >= np.arange(P)[None, :], np.ones((P, P))], 1)
    blocks = np.arange(P)[:, None] // NCP == np.arange(CM)[None, :]
    arrays = dict(x=x.reshape(SEQ, D), weights=weights, wgate=wgate, cmpw2=cmpw2, pe2=pe2, gpre=gpre, gpost=gpost,
                  convw=convw, rope=rope.astype(f32), ropec=ropec.astype(f32), cmask=cmask.astype(f32), blocks=blocks.astype(f32),
                  masks=masks.astype(f32), identf=np.eye(P, dtype=f32),
                  tri=tri.astype(f32))
    return {n: np.ascontiguousarray(v) for n, v in arrays.items()}


def kernel(**inputs):
    import concourse.bacc as bacc
    from concourse.bass_utils import run_bass_kernel_spmd

    arrays = lay_out(**{n: np.asarray(v) for n, v in inputs.items()})
    nc = bacc.Bacc("TRN2", target_bir_lowering=False, num_devices=1)
    args = {n: nc.dram_tensor(f"in_{n}", v.shape, mybir.dt.from_np(v.dtype), kind="ExternalInput").ap()
            for n, v in arrays.items()}
    out = nc.dram_tensor("out_0", (SEQ, D), F32, kind="ExternalOutput").ap()
    build(nc, out=out, **args)
    r = run_bass_kernel_spmd(nc, [{f"in_{n}": v for n, v in arrays.items()}], core_ids=[0])
    return r.results[0]["out_0"].reshape(1, SEQ, D)
```
